# Optimizing a Trainium2 kernel written in Bass

```python
import jax, jax.numpy as jnp
from jax import lax
import numpy as np

D_MODEL = 1024
BATCH = 1
SEQ = 512
DEPTH = 2
DEC_BATCH = 1
DEC_SEQ = 32
PAST_LEN = 256

CHUNK = 64
Q_BLOCK = 128
EPS = 1e-6

POOL_GROUPS = 4
POOL_GROUP_DIM = 64
POOL_WIDTH = POOL_GROUPS * POOL_GROUP_DIM
POOL_WINDOWS = (2, 4, 8, 16)
POOL_HIST = 15

MLA_HEADS = 8
MLA_Q_LORA = 256
MLA_KV_LORA = 128
MLA_NOPE = 64
MLA_ROPE = 32
MLA_V = 64
MLA_QK = MLA_NOPE + MLA_ROPE
ROPE_THETA = 10000.0

SB_HEADS = 4
SB_HEAD_DIM = 64
SB_WIDTH = SB_HEADS * SB_HEAD_DIM

N_BRANCH = 3
IN_SPLITS = (POOL_WIDTH, MLA_Q_LORA, MLA_KV_LORA, MLA_ROPE, SB_WIDTH, SB_WIDTH, SB_WIDTH, N_BRANCH * D_MODEL)
IN_COLS = POOL_WIDTH + MLA_Q_LORA + MLA_KV_LORA + MLA_ROPE + 3 * SB_WIDTH + N_BRANCH * D_MODEL

N_GROUPS = 4
EXPERTS_PER_GROUP = 4
N_EXPERTS = N_GROUPS * EXPERTS_PER_GROUP
TOP_K = 2
D_EXPERT = 256

kernel_name = "hybrid_streaming_encoder_step"

def rmsnorm(x, g):
    x32 = x.astype(jnp.float32)
    ms = jnp.mean(x32 * x32, axis=-1, keepdims=True)
    return (x32 * lax.rsqrt(ms + EPS)).astype(x.dtype) * g

def rope(x, pos):
    half = x.shape[-1] // 2
    inv = ROPE_THETA ** (-jnp.arange(half, dtype=jnp.float32) / half)
    ang = pos.astype(jnp.float32)[:, None] * inv[None, :]
    cos = jnp.cos(ang)[None, :, None, :]
    sin = jnp.sin(ang)[None, :, None, :]
    x1 = x[..., :half].astype(jnp.float32)
    x2 = x[..., half:].astype(jnp.float32)
    return jnp.concatenate([x1 * cos - x2 * sin, x1 * sin + x2 * cos], axis=-1).astype(x.dtype)

def split_cols(z, sizes):
    out, start = [], 0
    for n in sizes:
        out.append(z[..., start:start + n])
        start += n
    return out

def pool_mix(u_ext, pos, w_pool_lin, pool_scale):
    B, Lx, _ = u_ext.shape
    L = Lx - POOL_HIST
    cs = jnp.cumsum(u_ext.astype(jnp.float32), axis=1)
    cs = jnp.pad(cs, ((0, 0), (1, 0), (0, 0)))
    u = u_ext[:, POOL_HIST:]
    end = cs[:, POOL_HIST + 1:POOL_HIST + 1 + L]
    outs = []
    for g, w in enumerate(POOL_WINDOWS):
        sl = slice(g * POOL_GROUP_DIM, (g + 1) * POOL_GROUP_DIM)
        start = cs[:, POOL_HIST + 1 - w:POOL_HIST + 1 - w + L, sl]
        cnt = jnp.minimum(pos + 1, w).astype(jnp.float32)[None, :, None]
        mean = (end[..., sl] - start) / cnt
        outs.append(mean.astype(u.dtype) - u[..., sl])
    y = jnp.stack(outs, axis=2)
    y = jnp.einsum('blgc,gcd->blgd', y, w_pool_lin).reshape(B, L, POOL_WIDTH)
    return y * pool_scale

def mla_keys(lat, kr, p):
    B, K = lat.shape[:2]
    kv = (lat @ p["w_ukv"]).reshape(B, K, MLA_HEADS, MLA_NOPE + MLA_V)
    k_nope, v = kv[..., :MLA_NOPE], kv[..., MLA_NOPE:]
    k_rope = jnp.broadcast_to(kr[:, :, None, :], (B, K, MLA_HEADS, MLA_ROPE))
    k = rmsnorm(jnp.concatenate([k_nope, k_rope], axis=-1), p["g_qk_k"])
    return k, v

def attend_mla(q, q_pos, k, v, k_pos):
    s = jnp.einsum('bqhd,bkhd->bhqk', q, k).astype(jnp.float32) * (MLA_QK ** -0.5)
    mask = (k_pos[None, :] // CHUNK) <= (q_pos[:, None] // CHUNK)
    s = jnp.where(mask[None, None], s, -jnp.inf)
    w = jax.nn.softmax(s, axis=-1).astype(v.dtype)
    return jnp.einsum('bhqk,bkhd->bqhd', w, v)

def attend_stick_breaking(q, q_pos, k, v, k_pos):
    z = jnp.einsum('bqhd,bkhd->bhqk', q, k).astype(jnp.float32) * (SB_HEAD_DIM ** -0.5)
    mask = (k_pos[None, :] < q_pos[:, None])[None, None]
    log_beta = jax.nn.log_sigmoid(z)
    log_keep = jnp.where(mask, jax.nn.log_sigmoid(-z), 0.0)
    between = lax.cumsum(log_keep, axis=3, reverse=True) - log_keep
    a = jnp.where(mask, jnp.exp(log_beta + between), 0.0).astype(v.dtype)
    return jnp.einsum('bhqk,bkhd->bqhd', a, v)

def sweep_queries(attend, q, q_pos, k, v, k_pos):
    B, L = q.shape[:2]
    if L <= Q_BLOCK:
        return attend(q, q_pos, k, v, k_pos)
    nb = L // Q_BLOCK
    qb = jnp.moveaxis(q.reshape(B, nb, Q_BLOCK, *q.shape[2:]), 1, 0)
    pb = q_pos.reshape(nb, Q_BLOCK)
    o = lax.map(lambda a: attend(a[0], a[1], k, v, k_pos), (qb, pb))
    return jnp.moveaxis(o, 0, 1).reshape(B, L, *o.shape[3:])

def token_mixers(xn, pos, p, hist):
    B, L, _ = xn.shape
    u_pool, c_q, c_kv, k_r, q_sb, k_sb, v_sb, gate_pre = split_cols(xn @ p["w_in"], IN_SPLITS)
    pool_hist = jnp.zeros((B, POOL_HIST, POOL_WIDTH), xn.dtype) if hist is None else hist["pool"]
    u_ext = jnp.concatenate([pool_hist, u_pool], axis=1)
    y_pool = pool_mix(u_ext, pos, p["w_pool_lin"], p["pool_scale"])
    q = (rmsnorm(c_q, p["g_q_lora"]) @ p["w_uq"]).reshape(B, L, MLA_HEADS, MLA_QK)
    q = jnp.concatenate([q[..., :MLA_NOPE], rope(q[..., MLA_NOPE:], pos)], axis=-1)
    q = rmsnorm(q, p["g_qk_q"])
    lat_new = rmsnorm(c_kv, p["g_kv_lora"])
    kr_new = rope(k_r[:, :, None, :], pos)[:, :, 0, :]
    q_sb = q_sb.reshape(B, L, SB_HEADS, SB_HEAD_DIM)
    k_sb = k_sb.reshape(B, L, SB_HEADS, SB_HEAD_DIM)
    v_sb = v_sb.reshape(B, L, SB_HEADS, SB_HEAD_DIM)
    if hist is None:
        lat, kr, ksb, vsb = lat_new, kr_new, k_sb, v_sb
    else:
        lat = jnp.concatenate([hist["lat"], lat_new], axis=1)
        kr = jnp.concatenate([hist["kr"], kr_new], axis=1)
        ksb = jnp.concatenate([hist["sbk"], k_sb], axis=1)
        vsb = jnp.concatenate([hist["sbv"], v_sb], axis=1)
    k_pos = jnp.arange(lat.shape[1], dtype=jnp.int32)
    k_mla, v_mla = mla_keys(lat, kr, p)
    y_mla = sweep_queries(attend_mla, q, pos, k_mla, v_mla, k_pos).reshape(B, L, MLA_HEADS * MLA_V)
    y_sb = sweep_queries(attend_stick_breaking, q_sb, pos, ksb, vsb, k_pos).reshape(B, L, SB_WIDTH)
    g = jax.nn.sigmoid(gate_pre).reshape(B, L, N_BRANCH, D_MODEL)
    h = (g[:, :, 0] * (y_pool @ p["w_br_pool"])
         + g[:, :, 1] * (y_mla @ p["w_br_mla"])
         + g[:, :, 2] * (y_sb @ p["w_br_sb"]))
    state = (lat_new, kr_new, k_sb, v_sb, u_ext[:, -POOL_HIST:])
    return h @ p["w_out"], state

def hier_moe(xn, p):
    B, L, _ = xn.shape
    lg = (xn @ p["w_router_group"]).astype(jnp.float32) + p["b_router_group"]
    pg = jax.nn.softmax(lg, axis=-1)
    grp = jnp.argmax(lg, axis=-1)
    p_grp = jnp.take_along_axis(pg, grp[..., None], axis=-1)
    le = ((xn @ p["w_router_expert"]).astype(jnp.float32) + p["b_router_expert"]).reshape(B, L, N_GROUPS, EXPERTS_PER_GROUP)
    le_g = jnp.take_along_axis(le, grp[..., None, None], axis=2)[:, :, 0, :]
    top_v, top_i = lax.top_k(le_g, TOP_K)
    w_top = jax.nn.softmax(top_v, axis=-1) * p_grp
    expert_id = grp[..., None] * EXPERTS_PER_GROUP + top_i
    combine = jnp.sum(jax.nn.one_hot(expert_id, N_EXPERTS, dtype=jnp.float32) * w_top[..., None], axis=-2)
    combine = combine.astype(xn.dtype)
    out = jnp.zeros_like(xn)
    for e in range(N_EXPERTS):
        h = jax.nn.silu(xn @ p["w_exp_gate"][e]) * (xn @ p["w_exp_up"][e])
        out = out + combine[..., e:e + 1] * (h @ p["w_exp_down"][e])
    return out

def trunk_layer(x, pos, p, hist):
    mix, state = token_mixers(rmsnorm(x, p["g_mix_norm"]), pos, p, hist)
    x = x + mix
    x = x + hier_moe(rmsnorm(x, p["g_ffn_norm"]), p)
    return x, state

def setup_inputs(seed: int = 0) -> dict:
    key = jax.random.key(seed)
    ks = iter(jax.random.split(key, 32))
    f32 = jnp.float32

    def nrm(shape, scale):
        return jax.random.normal(next(ks), shape, f32) * scale

    def gain(shape):
        return 1.0 + 0.05 * jax.random.normal(next(ks), shape, f32)

    return {
        "x_prompt": nrm((BATCH, SEQ, D_MODEL), 1.0),
        "x_sample": nrm((DEC_BATCH, DEC_SEQ, D_MODEL), 1.0),
        "cache_mla_latent": nrm((DEPTH, DEC_BATCH, PAST_LEN, MLA_KV_LORA), 1.0),
        "cache_mla_krope": nrm((DEPTH, DEC_BATCH, PAST_LEN, MLA_ROPE), 1.0),
        "cache_sb_k": nrm((DEPTH, DEC_BATCH, PAST_LEN, SB_HEADS, SB_HEAD_DIM), 1.0),
        "cache_sb_v": nrm((DEPTH, DEC_BATCH, PAST_LEN, SB_HEADS, SB_HEAD_DIM), 1.0),
        "state_pool": nrm((DEPTH, DEC_BATCH, POOL_HIST, POOL_WIDTH), 1.0),
        "g_mix_norm": gain((DEPTH, D_MODEL)),
        "w_in": nrm((DEPTH, D_MODEL, IN_COLS), D_MODEL ** -0.5),
        "w_pool_lin": nrm((DEPTH, POOL_GROUPS, POOL_GROUP_DIM, POOL_GROUP_DIM), POOL_GROUP_DIM ** -0.5),
        "pool_scale": gain((DEPTH, POOL_WIDTH)),
        "g_q_lora": gain((DEPTH, MLA_Q_LORA)),
        "w_uq": nrm((DEPTH, MLA_Q_LORA, MLA_HEADS * MLA_QK), MLA_Q_LORA ** -0.5),
        "g_kv_lora": gain((DEPTH, MLA_KV_LORA)),
        "w_ukv": nrm((DEPTH, MLA_KV_LORA, MLA_HEADS * (MLA_NOPE + MLA_V)), MLA_KV_LORA ** -0.5),
        "g_qk_q": gain((DEPTH, MLA_QK)),
        "g_qk_k": gain((DEPTH, MLA_QK)),
        "w_br_pool": nrm((DEPTH, POOL_WIDTH, D_MODEL), POOL_WIDTH ** -0.5),
        "w_br_mla": nrm((DEPTH, MLA_HEADS * MLA_V, D_MODEL), (MLA_HEADS * MLA_V) ** -0.5),
        "w_br_sb": nrm((DEPTH, SB_WIDTH, D_MODEL), SB_WIDTH ** -0.5),
        "w_out": nrm((DEPTH, D_MODEL, D_MODEL), D_MODEL ** -0.5),
        "g_ffn_norm": gain((DEPTH, D_MODEL)),
        "w_router_group": nrm((DEPTH, D_MODEL, N_GROUPS), D_MODEL ** -0.5),
        "b_router_group": nrm((DEPTH, N_GROUPS), 0.01),
        "w_router_expert": nrm((DEPTH, D_MODEL, N_EXPERTS), D_MODEL ** -0.5),
        "b_router_expert": nrm((DEPTH, N_EXPERTS), 0.01),
        "w_exp_gate": nrm((DEPTH, N_EXPERTS, D_MODEL, D_EXPERT), D_MODEL ** -0.5),
        "w_exp_up": nrm((DEPTH, N_EXPERTS, D_MODEL, D_EXPERT), D_MODEL ** -0.5),
        "w_exp_down": nrm((DEPTH, N_EXPERTS, D_EXPERT, D_MODEL), D_EXPERT ** -0.5),
    }

def reference(x_prompt, x_sample, cache_mla_latent, cache_mla_krope, cache_sb_k, cache_sb_v, state_pool,
              g_mix_norm, w_in, w_pool_lin, pool_scale, g_q_lora, w_uq, g_kv_lora, w_ukv, g_qk_q, g_qk_k,
              w_br_pool, w_br_mla, w_br_sb, w_out, g_ffn_norm, w_router_group, b_router_group,
              w_router_expert, b_router_expert, w_exp_gate, w_exp_up, w_exp_down):
    past = cache_mla_latent.shape[2]
    pos_p = jnp.arange(x_prompt.shape[1], dtype=jnp.int32)
    pos_s = past + jnp.arange(x_sample.shape[1], dtype=jnp.int32)
    xp, xs = x_prompt, x_sample
    new_p = [[], [], [], [], []]
    new_s = [[], [], [], [], []]
    for l in range(DEPTH):
        p = {
            "g_mix_norm": g_mix_norm[l], "w_in": w_in[l], "w_pool_lin": w_pool_lin[l],
            "pool_scale": pool_scale[l], "g_q_lora": g_q_lora[l], "w_uq": w_uq[l],
            "g_kv_lora": g_kv_lora[l], "w_ukv": w_ukv[l], "g_qk_q": g_qk_q[l], "g_qk_k": g_qk_k[l],
            "w_br_pool": w_br_pool[l], "w_br_mla": w_br_mla[l], "w_br_sb": w_br_sb[l],
            "w_out": w_out[l], "g_ffn_norm": g_ffn_norm[l],
            "w_router_group": w_router_group[l], "b_router_group": b_router_group[l],
            "w_router_expert": w_router_expert[l], "b_router_expert": b_router_expert[l],
            "w_exp_gate": w_exp_gate[l], "w_exp_up": w_exp_up[l], "w_exp_down": w_exp_down[l],
        }
        hist = {"lat": cache_mla_latent[l], "kr": cache_mla_krope[l], "sbk": cache_sb_k[l],
                "sbv": cache_sb_v[l], "pool": state_pool[l]}
        xp, st_p = trunk_layer(xp, pos_p, p, None)
        xs, st_s = trunk_layer(xs, pos_s, p, hist)
        for i in range(5):
            new_p[i].append(st_p[i])
            new_s[i].append(st_s[i])
    return (xp, xs,
            jnp.stack(new_p[0]), jnp.stack(new_p[1]), jnp.stack(new_p[2]), jnp.stack(new_p[3]), jnp.stack(new_p[4]),
            jnp.stack(new_s[0]), jnp.stack(new_s[1]), jnp.stack(new_s[2]), jnp.stack(new_s[3]), jnp.stack(new_s[4]))


_drawn_inputs = setup_inputs


def setup_inputs(seed=0):
    import zlib

    import numpy as np

    out = dict(_drawn_inputs(seed))
    spreads = {}
    factors = {'g_q_lora': 3.501, 'g_qk_q': 4.592, 'g_qk_k': 3.696, 'b_router_expert': 4.154}
    for name, (base, spread) in spreads.items():
        noise = np.random.default_rng([zlib.crc32(name.encode()), seed]).standard_normal(out[name].shape)
        drawn = base * np.exp(spread * noise) if base else spread * noise
        out[name] = __import__('jax').numpy.asarray(drawn.astype(out[name].dtype))
    for name, factor in factors.items():
        out[name] = (out[name] * factor).astype(out[name].dtype)
    return out
```

```python
from contextlib import ExitStack

import numpy as np

import concourse.bass as bass
from concourse import mybir

F32 = mybir.dt.float32
F32R = mybir.dt.float32r
I32 = mybir.dt.int32
U32 = mybir.dt.uint32
ALU = mybir.AluOpType
ACT = mybir.ActivationFunctionType
AX = mybir.AxisListType.X
TABLE_LN_EXP = "natural_log_exp_and_others"
TABLE_SIGMOID = "sigmoid_and_others"

P = 128
D = 1024
DC = D // P
SEQ, DEC, PAST = 512, 32, 256
T = SEQ + DEC
HALF = T // 2
DEPTH = 2
EPS = 1e-6
TM = [128, 128, 128, 128, 32]
TO = [0, 128, 256, 384, 512]
NTILE = len(TM)
KM = TM + [128, 128]
KO = TO + [544, 672]
NKT = len(KM)
KEYS = SEQ + DEC + PAST
POOL_W, Q_LORA, KV_LORA, ROPE, SBW = 256, 256, 128, 32, 256
HIST = 15
WINDOWS = (2, 4, 8, 16)
C_POOL, C_Q, C_KV, C_KR = 0, 256, 512, 640
C_QS, C_KS, C_VS, C_GATE = 672, 928, 1184, 1440
HEADS, NOPE, VD, QK = 8, 64, 64, 96
SBH = 4
HR = ROPE // 2
NE, NG, EPG, DE = 16, 4, 4, 256
RING = 4
CHUNK = 2048
MIXC = 28
TILES = 24
UW = 16 + SEQ + 16 + DEC
UP, US = 16, 16 + SEQ + 16
SB_BLOCKS = [(0, 0, 0, 512), (512, 1, 128, 384), (896, 3, 384, 128), (1024, 2, 256, 256)]
SB_SAMPLE = [(1280, 5), (1312, 6), (1344, 4)]
SBC = 1376
NEG = -1e30
CONST_COLS = [("ID", P), ("NTRI", P), ("STRI", P), ("COS", 80), ("SIN", 80), ("INVC", 32), ("JL", 20), ("VALID", 20), ("STEP", 5), ("TILE", TILES)]
K_ID, K_NTRI, K_STRI, K_COS, K_SIN, K_INVC, K_JL, K_VALID, K_STEP, K_TILE = (
    sum(n for _, n in CONST_COLS[:i]) for i in range(len(CONST_COLS)))
NCONST = sum(n for _, n in CONST_COLS)
FILLS = 2
DVE_FILLS = 10
DVE_LINKS = 55


def at(sem_per, layer, n):
    return layer * sem_per[1] + (n + sem_per[2])


def hybrid_streaming_encoder(nc, A, out):
    ctx = ExitStack()
    with ctx:
        def sb(name, shape, dt=F32):
            return ctx.enter_context(nc.sbuf_tensor(name, shape, dt))

        def dram(name, shape, dt=F32):
            return nc.dram_tensor(name, shape, dt, kind="Internal").ap()

        def sem(name, per=0, start=0):
            return (ctx.enter_context(nc.semaphore(name)), per, start)

        wr = sb("wr", [P, RING, CHUNK])
        con = sb("con", [P, NCONST])
        lat = sb("lat", [P, NKT, KV_LORA])
        krt = sb("krt", [P, NKT, ROPE])
        rs = sb("rs", [P, T])
        small = sb("small", [P, 160])
        sums = sb("sums", [P, NTILE, HEADS])
        nmax = sb("nmax", [P, 3])
        kss = sb("kss", [P, 2, HEADS])
        gk_bc = sb("gk_bc", [P, KV_LORA])
        bias_bc = sb("bias_bc", [P, 20])
        hist = sb("hist", [16, POOL_W])
        wpl = sb("wpl", [P, 2, P])
        wrt = sb("wrt", [P, DC, 20])
        pool_out = sb("pool_out", [16, 4 * P])
        ones = sb("ones", [P, P])
        nones = sb("nones", [P, P])
        negrow = sb("negrow", [1, 64])
        halfrow = sb("halfrow", [1, P])
        rt = sb("rt", [P, 1412 + 16 + 80])
        ints = sb("ints", [P, TILES + 1], I32)
        slots = sb("slots", [P, 2 * NTILE], I32)

        shapes = {
            "x_ybr": [P, DC, T],
            "xn": [P, DC, T],
            "qt_ht": [P, DC, T],
            "big": [P, 8 * KEYS + 272],
            "ksv": [P, NKT, 2 * SBW],
            "qs": [P, 2, T],
            "kst": [P, 3 * T],
            "cqT": [P, 2, T],
            "lT": [P, KEYS],
            "vv": [P, NKT, HEADS * VD],
            "work": [P, 6144],
        }
        with ExitStack() as plain:
            (x_ybr, xn, qt_ht, big, ksv, qs, kst_, cqT, lT, vv, work) = (
                plain.enter_context(nc.sbuf_tensor(name, shape, F32)) for name, shape in shapes.items())
        x_r, xn_r, qt_r, big_r, ksv_r, qs_r, kst_r, cqT_r, lT_r, vv_r, work_r = (
            sb(f"{name}_r", shape, F32R) for name, shape in shapes.items())
        xT = ybr = x_ybr
        qT = qt_ht
        kst = kst_[:, 0:2 * KEYS].rearrange("p (m n) -> p m n", m=2)

        toka = big[:, 0:5 * 416].rearrange("p (t n) -> p t n", t=5)
        o = 5 * 416
        u = big[:, o:o + 2 * UW].rearrange("p (m n) -> p m n", m=2)
        sa = big[:, o + 2 * UW:o + 4 * UW].rearrange("p (m n) -> p m n", m=2)
        sb_ = big[:, o + 4 * UW:o + 6 * UW].rearrange("p (m n) -> p m n", m=2)
        yp = work[:, 4200:4200 + 2 * T].rearrange("p (m n) -> p m n", m=2)
        kT = big[:, 0:8 * KEYS].rearrange("p (h n) -> p h n", h=HEADS)
        xtok = big[:, 0:NTILE * D].rearrange("p (t n) -> p t n", t=NTILE)
        sq = work[:, 0:2 * 768].rearrange("p (s n) -> p s n", s=2)
        rope_t = work[:, 1536:1536 + 512].rearrange("p (a n) -> p a n", a=4)
        kw = work[:, 2048:2048 + 3 * HEADS * QK].rearrange("p (s n) -> p s n", s=3)
        zs = work[:, 0:SBC]
        sp_ = work[:, SBC:2 * SBC]
        aa = work[:, 2 * SBC:4 * SBC].rearrange("p (s n) -> p s n", s=2)
        pr = work[:, 0:1536].rearrange("p (s n) -> p s n", s=3)
        pt = work[:, 1536:2560].rearrange("p (s n) -> p s n", s=2)
        ot = work[:, 2560:3072]
        sg = work[:, 0:2 * T].rearrange("p (s n) -> p s n", s=2)
        acc = work[:, 2 * T:3 * T]
        tmp = work[:, 3 * T:4 * T]
        hsum = work[:, 4 * T:5 * T]
        xn_lo, ybr_lo = xn_r, x_r
        xn_hi = ([lT_r[:, 0:T], kst_r[:, 2 * T:3 * T], qs_r[:, 0, :], qs_r[:, 1, :]]
                 + [big_r[:, (8 + i) * T:(9 + i) * T] for i in range(4)])
        vv_rows = vv_r[:, :, :].rearrange("p t n -> p (t n)")
        ybr_hi = ([cqT_r[:, 0, :], cqT_r[:, 1, :]] + [vv_rows[:, i * T:i * T + T] for i in range(4)]
                  + [kst_r[:, i * T:i * T + T] for i in range(2)])
        hT_hi = qt_r
        hT_lo = big_r[:, 0:DC * T].rearrange("p (k n) -> p k n", k=DC)
        wsp = [ksv_r[:, :, :].rearrange("p t n -> p (t n)")[:, 0:3072], work_r[:, 3072:6144]]
        gate_hi, gate_lo = ([w[:, o:o + 1024].rearrange("p (k n) -> p k n", k=DC) for w in wsp] for o in (0, 1024))
        brw_hi, brw_lo = ([w[:, o:o + 512].rearrange("p (k n) -> p k n", k=4) for w in wsp] for o in (2048, 2560))
        SPLITS = ([(ybr[:, k, :], ybr_hi[k], ybr_lo[:, k, :]) for k in (0, 1)] + [(xn[:, 0, :], xn_hi[0], xn_lo[:, 0, :])]
                  + [(ybr[:, k, :], ybr_hi[k], ybr_lo[:, k, :]) for k in (6, 7)]
                  + [(xn[:, k, :], xn_hi[k], xn_lo[:, k, :]) for k in range(1, 8)]
                  + [(ybr[:, k, :], ybr_hi[k], ybr_lo[:, k, :]) for k in range(2, 6)])
        BR_K = [(0, 2), (2, 6), (6, 8)]
        logitT = work[0:20, 0:T]
        xg = work[:, 0:2048].rearrange("p (s n) -> p s n", s=2)
        xgT = work[:, 2048:4096].rearrange("p (s k n) -> p s k n", s=2, k=DC)
        hh = work[:, 4096:4608].rearrange("p (s n) -> p s n", s=2)
        ehT = work[:, 4608:5120].rearrange("p (s n) -> p s n", s=2)
        yo = work[:, 5120:6144]
        guw = [wr[:, 2 * s:2 * s + 2, :].rearrange("p a n -> p (a n)") for s in range(2)]
        g1 = xtok
        g2 = work[:, 0:NTILE * D].rearrange("p (t n) -> p t n", t=NTILE)
        down_w = [qt_ht[:, 4 * s:4 * s + 4, 0:512] for s in range(2)]

        ident = con[:, K_ID:K_ID + P]
        ntri = con[:, K_NTRI:K_NTRI + P]
        stri = con[:, K_STRI:K_STRI + P]
        cos = con[:, K_COS:K_COS + 80].rearrange("p (t n) -> p t n", t=5)
        sin = con[:, K_SIN:K_SIN + 80].rearrange("p (t n) -> p t n", t=5)
        invc = con[:, K_INVC:K_INVC + 32].rearrange("p (m n) -> p m n", m=2)
        G_MIX, G_FFN, G_PS, G_QL, G_Q, G_K, G_EPS = 0, 8, 16, 18, 20, 21, 22
        gains = small
        eps = small[:, G_EPS:G_EPS + 1]
        lss = small[:, 24:34]
        lrs = small[:, 34:44]
        ps = ctx.enter_context(nc.psum_tensor("ps", [P, 8, 512], F32))

        rows_d = dram("rows_d", [(TILES + 2) * P, D])
        row_tiles = rows_d.rearrange("(t p) n -> t p n", p=P)
        xres_d = dram("xres_d", [P, DC * T])

        j_less = con[:, K_JL:K_JL + 20].rearrange("p (t j) -> p t j", t=NTILE)
        valid = con[:, K_VALID:K_VALID + 20].rearrange("p (t j) -> p t j", t=NTILE)
        step128 = con[:, K_STEP:K_STEP + 5]
        tile_no = con[:, K_TILE:K_TILE + TILES]
        at_ = 0

        def cut(n, *shape):
            nonlocal at_
            ap = rt[:, at_:at_ + n]
            at_ += n
            if len(shape) == 2:
                ap = ap.rearrange("p (a b) -> p a b", a=shape[0])
            if len(shape) == 3:
                ap = ap.rearrange("p (a b c) -> p a b c", a=shape[0], b=shape[1])
            return ap

        r_lg, r_m, r_og, r_v, r_f = cut(100, 5, 20), cut(5), cut(20, 5, 4), cut(20, 5, 4), cut(5)
        r_eg, r_t16, r_le, r_m1, r_o1 = cut(20, 5, 4), cut(80, 5, 4, 4), cut(20, 5, 4), cut(5), cut(20, 5, 4)
        r_l2, r_m2, r_o2, r_e2, r_sum = cut(20, 5, 4), cut(5), cut(20, 5, 4), cut(5), cut(5)
        r_den, r_w1, r_w2 = cut(5), cut(5), cut(5)
        oh12, oh_both = cut(160, 2, 80), cut(96)
        r_cnt, r_th, r_nt, r_end, r_st = cut(96), cut(80, 16, 5), cut(16), cut(16), cut(16)
        r_pos, r_sl, r_slot = cut(80), cut(160, 2, 80), cut(10)
        r_te, r_ei = cut(16 * TILES, TILES, 16), cut(TILES)

        consts_in = sem("consts_in")
        rows_in = sem("rows_in")
        fills = sem("fills")
        dve_fills = sem("dve_fills")
        x_tr = sem("x_tr")
        x_in = sem("x_in", NTILE)
        w_in_ = [sem(f"w_loaded{s}", 96 if s == 3 else 96 + 4 * 32) for s in range(RING)]
        wbr_in = [sem(f"wbr_in{b}", 4 * 16) for b in range(3)]
        smalls = sem("smalls", 16 * 20)
        norm_sq = sem("norm_sq", 16)
        norm_mm = sem("norm_mm", 2)
        norm_ln = sem("norm_ln", 2)
        norm_rs = sem("norm_rs", 2)
        xn_rdy = sem("xn_rdy", 16)
        spill = sem("spill", 16)
        reload_ = sem("reload", 16)
        tk_mm = sem("tk_mm", 20)
        tk_ev = sem("tk_ev", 20)
        cm_mm = sem("cm_mm", 4)
        qs_ev = sem("qs_ev", 2)
        u_ev = sem("u_ev", 6)
        lss_rdy = sem("lss_rdy", 10)
        lrs_ln = sem("lrs_ln", 2)
        lrs_rdy = sem("lrs_rdy", 1)
        gpre = sem("gpre", 1)
        cq_n = sem("cq_n", 5)
        lat_n = sem("lat_n", 5)
        kr_n = sem("kr_n", 1)
        tp_mm = sem("tp_mm", 10)
        tp_ev = sem("tp_ev", 10)
        h_tr = sem("h_tr", 1)
        h_ev = sem("h_ev", 1)
        hz = sem("hz", 1)
        yp_rdy = sem("yp_rdy", 1)
        pl_mm = sem("pl_mm", 2)
        pl_ev = sem("pl_ev", 2)
        po_tr = sem("po_tr", 1)
        po_ev = sem("po_ev", 1)
        outs = sem("outs", 16 * 10, start=16)
        kq_mm = sem("kq_mm", 12)
        kq_cp = sem("kq_cp", 12)
        kq_raw = sem("kq_raw", 12)
        kq_sq = sem("kq_sq", 12)
        kq_ss = sem("kq_ss", 12)
        kq_ln = sem("kq_ln", 12)
        kq_rs = sem("kq_rs", 12)
        kq_n = sem("kq_n", 12)
        kq_tp = sem("kq_tp", 12)
        kq_ev = sem("kq_ev", 12)
        z_mm = sem("z_mm", SBH)
        z_abs = sem("z_abs", SBH)
        z_exp = sem("z_exp", SBH)
        z_ln = sem("z_ln", SBH)
        sp_raw = sem("sp_raw", SBH)
        sp_rdy = sem("sp_rdy", 3 * SBH)
        sfx_mm = sem("sfx_mm", SBH)
        a_raw = sem("a_raw", SBH)
        a_rdy = sem("a_rdy", 3 * SBH)
        sv_mm = sem("sv_mm", SBH)
        sv_ev = sem("sv_ev", 4)
        NU = NTILE * HEADS
        s_mm = sem("s_mm", NU)
        s_max = sem("s_max", NU)
        s_exp = sem("s_exp", NU)
        pt_mm = sem("pt_mm", NU)
        pt_ev = sem("pt_ev", NU)
        pv_mm = sem("pv_mm", NU)
        o_nrm = sem("o_nrm", NTILE)
        o_tr = sem("o_tr", NTILE)
        o_ev = sem("o_ev", NTILE)
        sp_hi = sem("sp_hi", 16)
        sp_lo = sem("sp_lo", 16)
        g_hi = sem("g_hi", 32)
        g_lo = sem("g_lo", 32, start=3)
        b_hi = sem("b_hi", 24)
        b_lo = sem("b_lo", 24, start=3)
        h_sum = sem("h_sum", DC)
        h_hi = sem("h_hi", DC)
        h_lo = sem("h_lo", DC)
        br_mm = sem("br_mm", 24, start=2)
        br_sg = sem("br_sg", 24)
        br_pr = sem("br_pr", 24, start=2)
        br_ac = sem("br_ac", 8)
        wo_mm = sem("wo_mm", 8)
        x_mid = sem("x_mid", 8)
        rt_mm = sem("rt_mm", 1)
        lg_ev = sem("lg_ev", 1)
        lg_tr = sem("lg_tr", 1)
        xt_mm = sem("xt_mm", NTILE)
        xt_ev = sem("xt_ev", NTILE)
        dve_link = sem("dve_link", DVE_LINKS)
        rt_e = sem("rt_e", 2)
        rt_x = sem("rt_x", 2)
        oh_rdy = sem("oh_rdy", 1)
        rk_mm = sem("rk_mm", 1)
        slots_rdy = sem("slots_rdy", 1)
        route = sem("route", 1)
        xs_wr = sem("xs_wr", 16 * 2 * NTILE)
        xs_zero = sem("xs_zero")
        gu_in = [sem(f"gu_in{s}") for s in range(2)]
        dn_in = [sem(f"dn_in{s}") for s in range(2)]
        xg_in = [sem(f"xg_in{s}") for s in range(2)]
        xg_tr = sem("xg_tr")
        xg_ev = sem("xg_ev")
        gu_mm = sem("gu_mm", start=2)
        eh_sg = sem("eh_sg")
        eh_g = sem("eh_g")
        eh_h = sem("eh_h")
        eh_tr = sem("eh_tr")
        eh_ev = sem("eh_ev")
        dn_mm = sem("dn_mm", start=2)
        yo_ev = sem("yo_ev", start=2)
        ys_wr = sem("ys_wr", start=16)
        gath = [sem(f"gath{t}", 32) for t in range(NTILE)]
        cb_1 = sem("cb_1", NTILE, start=1)
        cb_2 = sem("cb_2", NTILE)
        cb_tr = sem("cb_tr", NTILE)
        y_tr = sem("y_tr")
        y_ev = sem("y_ev")
        y_out = sem("y_out")
        passed = {eng.engine: sem(f"passed_{name}") for name, eng in (
            ("sync", nc.sync), ("gpsimd", nc.gpsimd), ("tensor", nc.tensor), ("scalar", nc.scalar), ("vector", nc.vector))}
        block = ctx.enter_context(nc.Block())

        def wait(eng, s, l, n):
            eng.wait_ge(s[0], at(s, l, n))

        def starts(eng, *sems):
            for s in sems:
                eng.sem_inc(s[0], s[2])

        def stand(eng):
            eng.sem_inc(passed[eng.engine][0], 1)

        def row(ap2, l):
            return ap2[bass.ds(l, 1)]

        NT, NR = TILES, TILES + 2

        def f32(ap):
            return ap.bitcast(F32)

        def pair_done(l, it):
            return l * (NT * 16) + it * 32 + ys_wr[2]

        def pass_pair(eng, l, it, *counts):
            eng.wait_ge(dn_mm[0], l * NT + it * 2 + dn_mm[2])
            for s, n in counts:
                eng.sem_inc(s[0], n)

        def pairs_in_use(eng, l):
            wait(eng, route, l, 1)
            stand(eng)
            return eng.value_load(ints[0:1, TILES:TILES + 1], min_val=1, max_val=NT // 2)

        @block.sync
        def _(sp):
            starts(sp, outs)
            sp.dma_start(con[:, :], A["con"]).then_inc(consts_in[0], 16)
            sp.dma_start(xtok[:, 0:4, :], A["x_prompt"].rearrange("b (t p) n -> p (b t) n", p=P)).then_inc(rows_in[0], 16)
            sp.dma_start(xtok[0:DEC, 4, :], A["x_sample"].rearrange("b p n -> p (b n)")).then_inc(rows_in[0], 16)
            with sp.Fori(0, DEPTH) as l:
                used = [(tk_mm, 5), (tk_mm, 10), (tk_mm, 15), (tk_mm, 20), (cm_mm, 2), (cm_mm, 4), (kq_mm, 7), (kq_mm, 12)]

                def mat(name):
                    return row(A[name], l)

                def chunk(c, base, pieces, extra=None):
                    s = c % RING
                    if RING <= c < 8:
                        wait(sp, used[c - RING][0], l, used[c - RING][1])
                        stand(sp)
                    for dst, src in pieces:
                        sp.dma_start(dst, src).then_inc(w_in_[s][0], 16)

                def cols(c, name, lo, n):
                    s = c % RING
                    w = wr[:, s, 0:8 * n].rearrange("p (k n) -> p k n", k=DC)
                    src = mat(name)[:, :, lo:lo + n].rearrange("o (k p) n -> p (o k) n", p=P)
                    chunk(c, 0, [(w[:, 0:4], src[:, 0:4]), (w[:, 4:8], src[:, 4:8])])

                sp.wait_ge(ys_wr[0], l * (NT * 16) + ys_wr[2])
                sp.wait_ge(dve_fills[0], DVE_FILLS)
                with nc.allow_non_contiguous_dma(reason="gains are a few hundred elements"):
                    n_small = 0

                    def load(dst, src):
                        nonlocal n_small
                        n_small += 1
                        sp.dma_start(dst, src).then_inc(smalls[0], 16)

                    load(gains[:, G_MIX:G_MIX + 8], mat("g_mix_norm").rearrange("o (k p) -> p (o k)", p=P))
                    load(gains[:, G_FFN:G_FFN + 8], mat("g_ffn_norm").rearrange("o (k p) -> p (o k)", p=P))
                    load(gains[:, G_PS:G_PS + 2], mat("pool_scale").rearrange("o (k p) -> p (o k)", p=P))
                    load(gains[:, G_QL:G_QL + 2], mat("g_q_lora").rearrange("o (k p) -> p (o k)", p=P))
                    load(gains[0:QK, G_Q:G_Q + 1], mat("g_qk_q").rearrange("o p -> p o"))
                    load(gains[0:QK, G_K:G_K + 1], mat("g_qk_k").rearrange("o p -> p o"))
                    load(gk_bc[:, :], mat("g_kv_lora").to_broadcast([P, KV_LORA]))
                    load(bias_bc[:, 0:4], mat("b_router_group").to_broadcast([P, 4]))
                    load(bias_bc[:, 4:20], mat("b_router_expert").to_broadcast([P, 16]))
                    load(wrt[:, :, 0:4], mat("w_router_group").rearrange("o (k p) n -> p (o k) n", p=P))
                    load(wrt[:, :, 4:20], mat("w_router_expert").rearrange("o (k p) n -> p (o k) n", p=P))
                    for g in range(4):
                        load(wpl[64 * (g % 2):64 * (g % 2) + 64, g // 2, 64 * (g % 2):64 * (g % 2) + 64],
                             mat("w_pool_lin")[:, g].rearrange("o c d -> c (o d)"))
                    load(hist[1:16, :], mat("state_pool").rearrange("o b t c -> (o b t) c"))
                    load(lat[:, 5:7, :], mat("cache_mla_latent").rearrange("o b (t p) n -> p (o b t) n", p=P))
                    load(krt[:, 5:7, :], mat("cache_mla_krope").rearrange("o b (t p) n -> p (o b t) n", p=P))
                    load(ksv[:, 5:7, 0:256], mat("cache_sb_k").rearrange("o b (t p) h n -> p (o b t) (h n)", p=P))
                    load(ksv[:, 5:7, 256:512], mat("cache_sb_v").rearrange("o b (t p) h n -> p (o b t) (h n)", p=P))
                    assert n_small == 20, n_small
                wait(sp, cb_1, l, 0)
                for c, lo, n in ((0, C_Q, 256), (1, C_KV, 160), (2, C_KS, 256), (3, C_VS, 256)):
                    cols(c, "w_in", lo, n)
                wait(sp, x_in, l, NTILE)
                sp.dma_start(xres_d, xT[:, :, :].rearrange("p k t -> p (k t)")).then_inc(spill[0], 16)
                cols(4, "w_in", C_QS, 256)
                cols(5, "w_in", C_POOL, 256)
                ukv = row(A["w_ukv"], l).rearrange("o p n -> p (o n)")
                chunk(6, 0, [(wr[:, 2, 512 * a:512 * a + 512], ukv[:, 512 * a:512 * a + 512]) for a in range(2)])
                uq = row(A["w_uq"], l).rearrange("o (k p) n -> p (o k) n", p=P)
                chunk(7, 0, [(wr[:, 3, 768 * a:768 * a + 768], uq[:, a]) for a in range(2)])
                wait(sp, lat_n, l, 5)
                sp.dma_start(row(out["lat_p"], l).rearrange("o b (t p) n -> p (o b t) n", p=P), lat[:, 0:4, :]).then_inc(outs[0], 16)
                sp.dma_start(row(out["lat_s"], l).rearrange("o b p n -> p (o b n)"), lat[0:DEC, 4, :]).then_inc(outs[0], 16)
                wait(sp, kr_n, l, 1)
                sp.dma_start(row(out["kr_p"], l).rearrange("o b (t p) n -> p (o b t) n", p=P), krt[:, 0:4, :]).then_inc(outs[0], 16)
                sp.dma_start(row(out["kr_s"], l).rearrange("o b p n -> p (o b n)"), krt[0:DEC, 4, :]).then_inc(outs[0], 16)
                wait(sp, tk_ev, l, 20)
                for nm, c in (("sbk", 0), ("sbv", 256)):
                    sp.dma_start(row(out[nm + "_p"], l).rearrange("o b (t p) h n -> p (o b t) (h n)", p=P),
                                 ksv[:, 0:4, c:c + 256]).then_inc(outs[0], 16)
                    sp.dma_start(row(out[nm + "_s"], l).rearrange("o b p h n -> p (o b h n)"),
                                 ksv[0:DEC, 4, c:c + 256]).then_inc(outs[0], 16)
                wait(sp, po_ev, l, 1)
                for nm, c in (("pool_p", 0), ("pool_s", 256)):
                    sp.dma_start(row(out[nm], l).rearrange("o b t c -> (o b t) c"),
                                 pool_out[1:16, c:c + 256]).then_inc(outs[0], 16)
                with sp.Fori(0, 4) as dp:
                    for b, (nm, k0, k1) in enumerate((("w_br_pool", 0, 2), ("w_br_mla", 2, 6), ("w_br_sb", 6, 8))):
                        if b == 0:
                            wait(sp, kq_mm, l, 12)
                        sp.wait_ge(g_lo[0], l * g_lo[1] + dp * 6 + (b - 2 + g_lo[2]))
                        w = wr[:, b, :].rearrange("p (k n) -> p k n", k=DC)
                        src = mat("w_in")[:, :, bass.ds(dp * 256 + (C_GATE + D * b), 256)].rearrange("o (k p) n -> p (o k) n", p=P)
                        sp.dma_start(w[:, 0:4], src[:, 0:4]).then_inc(w_in_[b][0], 16)
                        sp.dma_start(w[:, 4:8], src[:, 4:8]).then_inc(w_in_[b][0], 16)
                        sp.wait_ge(b_lo[0], l * b_lo[1] + dp * 6 + (b - 2 + b_lo[2]))
                        w = wr[:, 3, :].rearrange("p (k n) -> p k n", k=DC)
                        sp.dma_start(w[:, k0:k1], mat(nm)[:, :, bass.ds(dp * 256, 256)].rearrange("o (k p) n -> p (o k) n", p=P)).then_inc(wbr_in[b][0], 16)
                for c in range(4):
                    if c < 3:
                        wait(sp, g_lo, l, 22 + c)
                    else:
                        wait(sp, b_lo, l, 24)
                    stand(sp)
                    cols(24 + c, "w_out", 256 * c, 256)
                wait(sp, br_mm, l, 24)
                stand(sp)
                wait(sp, spill, l, 16)
                sp.dma_start(xT[:, :, :].rearrange("p k t -> p (k t)"), xres_d).then_inc(reload_[0], 16)

                pairs = pairs_in_use(sp, l)
                wait(sp, xs_wr, l, 16 * 2 * NTILE)

                def load_rows(s, t):
                    sp.dma_start(xg[:, s, :], row_tiles[bass.ds(t, 1)].rearrange("o p n -> p (o n)")).then_inc(xg_in[s][0], 16)

                load_rows(0, 0)
                load_rows(1, 1)
                with sp.Fori(0, NT // 2) as it:
                    with sp.If(it < pairs):
                        for s in range(2):
                            e = sp.value_load(ints[0:1, bass.ds(it * 2 + s, 1)], min_val=0, max_val=NE - 1)
                            sp.wait_ge(gu_mm[0], l * NT + it * 2 + (s - 1 + gu_mm[2]))
                            g = guw[s].rearrange("p (k m n) -> p k m n", k=DC, m=2)
                            for m, nm in enumerate(("w_exp_gate", "w_exp_up")):
                                src = A[nm].rearrange("l e r c -> (l e) r c")[bass.ds(l * NE + e, 1)]
                                sp.dma_start(g[:, :, m], src.rearrange("o (k p) n -> p (o k) n", p=P)).then_inc(gu_in[s][0], 16)
                            sp.wait_ge(xg_tr[0], l * NR + it * 2 + (s + 1))
                            load_rows(s, it * 2 + (s + 2))
                            sp.wait_ge(dn_mm[0], l * NT + it * 2 + (s - 1 + dn_mm[2]))
                            src = A["w_exp_down"].rearrange("l e r c -> (l e) r c")[bass.ds(l * NE + e, 1)]
                            d = down_w[s].rearrange("p (k a) n -> p k a n", k=2)
                            for k in range(2):
                                sp.dma_start(d[:, k], src[:, P * k:P * k + P].rearrange("o p (a n) -> p (o a) n", a=2)).then_inc(dn_in[s][0], 16)
                    with sp.Else():
                        pass_pair(sp, l, it, (gu_in[0], 32), (gu_in[1], 32), (dn_in[0], 32), (dn_in[1], 32), (xg_in[0], 16), (xg_in[1], 16))
            sp.wait_ge(y_ev[0], NTILE)
            sp.dma_start(out["y_p"].rearrange("b (t p) n -> p (b t) n", p=P), xtok[:, 0:4, :]).then_inc(y_out[0], 16)
            sp.dma_start(out["y_s"].rearrange("b p n -> p (b n)"), xtok[0:DEC, 4, :]).then_inc(y_out[0], 16)
            sp.wait_ge(y_out[0], 32)
            sp.wait_ge(outs[0], DEPTH * 160 + outs[2])

        @block.gpsimd
        def _(pool):
            nc.gpsimd.memset(halfrow[:, 0:64], 1.0).then_inc(fills[0], 1)
            nc.gpsimd.memset(halfrow[:, 64:128], 0.0).then_inc(fills[0], 1)
            pool.wait_ge(cm_mm[0], 4)
            for t in range(TILES + 2):
                pool.dma_start(rows_d[t * P:(t + 1) * P, :], A["zeros"]).then_inc(xs_zero[0], 16)
            with pool.Fori(0, DEPTH) as l:
                for h in range(SBH):
                    for src, raw, rdy in ((sp_, sp_raw, sp_rdy), (aa[:, h % 2], a_raw, a_rdy)):
                        wait(pool, raw, l, h + 1)
                        stand(pool)
                        d = src[:, 0:1024].rearrange("p (b n) -> p b n", b=2)[:, :, 0:P]
                        nc.gpsimd.affine_select(out=d, in_=d, compare_op=ALU.is_gt, fill=0.0, base=0,
                                                pattern=[[0, 2], [1, P]], channel_multiplier=-1).then_inc(rdy[0], 1)
                        d = src[:, 896:1152]
                        nc.gpsimd.affine_select(out=d.rearrange("p (b n) -> p b n", b=2), in_=d.rearrange("p (b n) -> p b n", b=2),
                                                compare_op=ALU.is_gt, fill=0.0, base=0,
                                                pattern=[[0, 2], [1, P]], channel_multiplier=-1).then_inc(rdy[0], 1)
                        d = src[:, 1344:1376]
                        nc.gpsimd.affine_select(out=d, in_=d, compare_op=ALU.is_gt, fill=0.0, base=0,
                                                pattern=[[1, 32]], channel_multiplier=-1).then_inc(rdy[0], 1)
                pool.wait_ge(xs_zero[0], 16 * (TILES + 2))
                wait(pool, slots_rdy, l, 1)
                for t in range(NTILE):
                    wait(pool, xt_ev, l, t + 1)
                    stand(pool)
                    for w in range(2):
                        pool.indirect_dma_start(
                            rows_d, bass.IndirectOffsetOnAxis(ap=slots[0:TM[t], w * NTILE + t:w * NTILE + t + 1], axis=0),
                            xtok[0:TM[t], t, :], None).then_inc(xs_wr[0], 16)
                pool.wait_ge(ys_wr[0], pair_done(l + 1, 0))
                pool.wait_ge(xg_ev[0], (l + 1) * NR)
                stand(pool)
                for t in range(NTILE):
                    for w, g in enumerate((g1, g2)):
                        pool.indirect_dma_start(
                            g[0:TM[t], t, :], None, rows_d,
                            bass.IndirectOffsetOnAxis(ap=slots[0:TM[t], w * NTILE + t:w * NTILE + t + 1], axis=0)).then_inc(gath[t][0], 16)

        @block.tensor
        def _(pe):
            mm = nc.tensor.matmul
            starts(pe, br_mm, gu_mm, dn_mm)
            pe.wait_ge(consts_in[0], 16)
            pe.wait_ge(rows_in[0], 32)

            def bank(b, n=512, m=P, lo=0):
                return ps[0:m, b, lo:lo + n]

            for t in range(NTILE):
                if t >= 4:
                    pe.wait_ge(x_in[0], t - 3)
                for k in range(DC):
                    ins = nc.tensor.transpose(bank(2 * (t % 4) + k // 4, TM[t], P, (k % 4) * P),
                                              xtok[0:TM[t], t, k * P:(k + 1) * P], ident[0:TM[t], 0:TM[t]])
                ins.then_inc(x_tr[0], 1)
            pe.wait_ge(dve_fills[0], DVE_FILLS)

            with pe.Fori(0, DEPTH) as l:
                def loaded(c):
                    s, n = c % RING, c // RING
                    wait(pe, w_in_[s], l, 32 * (n + 1) if c < 8 else w_in_[s][1])
                    return s

                def norm(w):
                    b = (6, 0)[w]
                    if w:
                        wait(pe, x_mid, l, 5)
                    for k in range(DC):
                        wait(pe, norm_sq, l, 8 * w + k + 1)
                        for h in range(2):
                            ins = mm(bank(b + h, HALF), ones[:, :], xn[:, k, h * HALF:(h + 1) * HALF],
                                     start=(k == 0), stop=(k == DC - 1))
                    ins.then_inc(norm_mm[0], 1)

                norm(0)
                for c, n in enumerate((256, 160, 256, 256)):
                    s = loaded(c)
                    w = wr[:, s, 0:8 * n].rearrange("p (k n) -> p k n", k=DC)
                    for t in range(NTILE):
                        g = c * NTILE + t
                        if g >= 6:
                            wait(pe, tk_ev, l, g - 5)
                        for k in range(DC):
                            if g == 0:
                                wait(pe, xn_rdy, l, k + 1)
                            ins = mm(bank(g % 6, n, TM[t]), xn[:, k, TO[t]:TO[t] + TM[t]], w[:, k, :],
                                     start=(k == 0), stop=(k == DC - 1))
                        ins.then_inc(tk_mm[0], 1)
                wait(pe, tk_ev, l, 20)
                for c in (4, 5):
                    s = loaded(c)
                    w = wr[:, s, :].rearrange("p (k n) -> p k n", k=DC)
                    for m in range(2):
                        b = 2 * ((c - 4) * 2 + m)
                        for k in range(DC):
                            for h in range(2):
                                ins = mm(bank(b + h, HALF), w[:, k, P * m:P * m + P], xn[:, k, h * HALF:(h + 1) * HALF],
                                         start=(k == 0), stop=(k == DC - 1), skip_group_check=True)
                        ins.then_inc(cm_mm[0], 1)

                wait(pe, u_ev, l, 6)
                wait(pe, qs_ev, l, 2)
                wait(pe, smalls, l, 320)
                wait(pe, hz, l, 1)
                stand(pe)
                for m in range(2):
                    ins = nc.tensor.transpose(bank(7, 16, P, 16 * m), hist[0:16, P * m:P * m + P], ident[0:16, 0:16])
                ins.then_inc(h_tr[0], 1)
                g = 0

                def group(src, tiles):
                    nonlocal g
                    if g >= 6:
                        wait(pe, tp_ev, l, g - 5)
                        stand(pe)
                    lo = 0
                    for t in tiles:
                        ins = nc.tensor.transpose(bank(g % 6, KM[t], P, lo), src(t), ident[0:KM[t], 0:KM[t]])
                        lo += KM[t]
                    ins.then_inc(tp_mm[0], 1)
                    g += 1

                for m in range(2):
                    for tiles in (range(4), range(4, 7)):
                        group(lambda t: ksv[0:KM[t], t, P * m:P * m + P], tiles)
                wait(pe, lat_n, l, 5)
                for tiles in (range(4), range(4, 7)):
                    group(lambda t: lat[0:KM[t], t, :], tiles)
                wait(pe, cq_n, l, 5)
                for m in range(2):
                    for tiles in (range(4), range(4, 5)):
                        group(lambda t: toka[0:KM[t], t, P * m:P * m + P], tiles)
                wait(pe, yp_rdy, l, 1)
                wait(pe, h_ev, l, 1)
                for m in range(2):
                    ins = nc.tensor.transpose(bank(7, P, 16, P * m), u[:, m, UP + SEQ - 16:UP + SEQ], ident)
                    ins = nc.tensor.transpose(bank(7, P, 16, 256 + P * m), u[:, m, US + DEC - 16:US + DEC], ident)
                ins.then_inc(po_tr[0], 1)
                wait(pe, tp_ev, l, 10)
                for m in range(2):
                    for h in range(2):
                        ins = mm(bank(2 * m + h, HALF), wpl[:, m, :], yp[:, m, h * HALF:(h + 1) * HALF], start=True, stop=True)
                    ins.then_inc(pl_mm[0], 1)

                wait(pe, pl_ev, l, 2)
                wait(pe, po_ev, l, 1)

                def kq_products(n):
                    b = 2 * (n % 2)
                    if n >= 2:
                        wait(pe, kq_raw, l, n - 1)
                    if n < 7:
                        t, m = n, KM[n]
                        if n == 0:
                            loaded(6)
                        for h in range(2):
                            ins = mm(bank(b + h, 512, m), lT[:, KO[t]:KO[t] + m], wr[:, 2, 512 * h:512 * h + 512], start=True, stop=True)
                    else:
                        t, m = n - 7, TM[n - 7]
                        if n == 7:
                            loaded(7)
                        for h in range(2):
                            for k in range(2):
                                ins = mm(bank(b + h, 384, m), cqT[:, k, TO[t]:TO[t] + m],
                                         wr[:, 3, 768 * k + 384 * h:768 * k + 384 * h + 384], start=(k == 0), stop=(k == 1))
                    ins.then_inc(kq_mm[0], 1)

                kq_products(0)
                kq_products(1)
                for n in range(12):
                    if n < 10:
                        kq_products(n + 2)
                    m = KM[n] if n < 7 else TM[n - 7]
                    wait(pe, kq_n, l, n + 1)
                    if n >= 2:
                        wait(pe, kq_ev, l, n - 1)
                    if m < P:
                        stand(pe)
                    for h in range(HEADS):
                        ins = nc.tensor.transpose(bank(4 + 2 * (n % 2) + h // 4, m, QK, P * (h % 4)),
                                                  kw[0:m, n % 3, QK * h:QK * h + QK], ident[0:m, 0:m])
                    ins.then_inc(kq_tp[0], 1)

                wait(pe, kq_ev, l, 12)
                wait(pe, kq_raw, l, 12)
                zf = ps[:, :, :].rearrange("p b n -> p (b n)")

                def zcol(h, lo, n, m=P):
                    return zf[0:m, 1536 * (h % 2) + lo:1536 * (h % 2) + lo + n]

                def z_products(h):
                    t, pb = h // 2, 64 * (h % 2)
                    if h >= 2:
                        wait(pe, a_raw, l, h - 1)
                    for lo, kt_, q0, nq in SB_BLOCKS:
                        mm(zcol(h, lo, nq), kst[pb:pb + 64, t, KO[kt_]:KO[kt_] + P], qs[pb:pb + 64, t, q0:q0 + nq],
                           start=(lo in (0, 512, 1024)), stop=True, skip_group_check=True)
                    for lo, kt_ in SB_SAMPLE:
                        ins = mm(zcol(h, lo, DEC), kst[pb:pb + 64, t, KO[kt_]:KO[kt_] + P], qs[pb:pb + 64, t, SEQ:T],
                                 start=False, stop=True, skip_group_check=True)
                    ins.then_inc(z_mm[0], 1)

                def add(h, w, lo, src, n):
                    return mm(zcol(h, lo, n), w, sp_[:, src:src + n], start=False, stop=True, skip_group_check=True)

                def suffix(h):
                    wait(pe, sp_rdy, l, 3 * h + 3)
                    w1, wa = ntri, nones[:, :]
                    for lo, n in ((0, 512), (512, 384), (896, 128), (1024, 256), (1280, 32), (1312, 32), (1344, 32)):
                        add(h, w1, lo, lo, n)
                    add(h, wa, 128, 512, 384)
                    add(h, wa, 256, 1024, 256)
                    add(h, wa, 384, 896, 128)
                    add(h, wa, 512 + 128, 1024, 256)
                    add(h, wa, 512 + 256, 896, 128)
                    add(h, wa, 1024 + 128, 896, 128)
                    add(h, wa, 1280, 1312, 32)
                    add(h, wa, 1280, 1344, 32)
                    ins = add(h, wa, 1312, 1344, 32)
                    ins.then_inc(sfx_mm[0], 1)

                def sb_values(h):
                    wait(pe, a_rdy, l, 3 * h + 3)
                    a_ = aa[:, h % 2]
                    pb = 64 * (h % 2)
                    if h == 2:
                        wait(pe, sv_ev, l, 2)
                    v = 256 + 64 * h
                    for i, (lo, kt_, q0, nq) in enumerate(SB_BLOCKS):
                        mm(ps[pb:pb + 64, 6, q0:q0 + nq], ksv[:, kt_, v:v + 64], a_[:, lo:lo + nq],
                           start=(i == 0), stop=(i == 3), skip_group_check=True)
                    for i, (lo, kt_) in enumerate(SB_SAMPLE):
                        m = KM[kt_]
                        ins = mm(ps[pb:pb + 64, 7, 0:DEC], ksv[0:m, kt_, v:v + 64], a_[0:m, lo:lo + DEC],
                                 start=(i == 0), stop=(i == 2), skip_group_check=True)
                    ins.then_inc(sv_mm[0], 1)

                z_products(0)
                z_products(1)
                for h in range(SBH):
                    suffix(h)
                    if h:
                        sb_values(h - 1)
                    if h + 2 < SBH:
                        z_products(h + 2)
                sb_values(SBH - 1)

                wait(pe, sv_ev, l, 4)
                pe.wait_ge(fills[0], FILLS)

                def scores(n):
                    t, h = n // HEADS, n % HEADS
                    if n >= 3:
                        wait(pe, s_exp, l, n - 2)
                    m = TM[t]
                    q = qT[0:QK, h, TO[t]:TO[t] + m]
                    if t < 4:
                        nk = P * (t + 1)
                        mm(bank(n % 3, nk), q, kT[0:QK, h, 0:nk], start=True, stop=False, skip_group_check=True)
                        ins = mm(bank(n % 3, 64, P, nk - 64), halfrow[:, :], negrow[:, :], start=False, stop=True, skip_group_check=True)
                    else:
                        ins = mm(bank(n % 3, 288, m), q, kT[0:QK, h, SEQ:KEYS], start=True, stop=True)
                    ins.then_inc(s_mm[0], 1)

                def turn(n):
                    t = n // HEADS
                    wait(pe, s_exp, l, n + 1)
                    if n >= 2:
                        wait(pe, pt_ev, l, n - 1)
                    if t == 4:
                        stand(pe)
                    if t < 4:
                        for j in range(t + 1):
                            ins = nc.tensor.transpose(bank(3 + n % 2, P, P, P * j), pr[:, n % 3, P * j:P * j + P], ident)
                    else:
                        for j, lo in ((1, 32), (2, 160)):
                            nc.tensor.transpose(bank(3 + n % 2, DEC, P, DEC * j), pr[0:DEC, n % 3, lo:lo + P], ident[0:DEC, 0:DEC])
                        ins = nc.tensor.transpose(bank(3 + n % 2, DEC, DEC, 0), pr[0:DEC, n % 3, 0:DEC], ident[0:DEC, 0:DEC])
                    ins.then_inc(pt_mm[0], 1)

                def values(n):
                    t, h = n // HEADS, n % HEADS
                    wait(pe, pt_ev, l, n + 1)
                    if h == 0 and t >= 2:
                        wait(pe, o_nrm, l, t - 1)
                    dst = ps[0:TM[t], 5 + t % 2, 64 * h:64 * h + 64]
                    if t < 4:
                        for j in range(t + 1):
                            ins = mm(dst, pt[:, n % 2, P * j:P * j + P], vv[:, j, 64 * h:64 * h + 64], start=(j == 0), stop=(j == t))
                    else:
                        for j in (1, 2):
                            mm(dst, pt[:, n % 2, DEC * j:DEC * j + DEC], vv[:, 4 + j, 64 * h:64 * h + 64], start=(j == 1), stop=False)
                        ins = mm(dst, pt[0:DEC, n % 2, 0:DEC], vv[0:DEC, 4, 64 * h:64 * h + 64], start=False, stop=True)
                    ins.then_inc(pv_mm[0], 1)

                def turn_out(t):
                    wait(pe, o_nrm, l, t + 1)
                    if t:
                        wait(pe, o_ev, l, t)
                    if t == 4:
                        stand(pe)
                    for j in range(4):
                        ins = nc.tensor.transpose(bank(7, TM[t], P, P * j), ot[0:TM[t], P * j:P * j + P], ident[0:TM[t], 0:TM[t]])
                    ins.then_inc(o_tr[0], 1)

                scores(0)
                scores(1)
                for n in range(NU):
                    if n + 2 < NU:
                        scores(n + 2)
                    if n >= 1:
                        values(n - 1)
                    turn(n)
                    if n % HEADS == 2 and n > HEADS:
                        turn_out(n // HEADS - 1)
                values(NU - 1)
                turn_out(NTILE - 1)

                wait(pe, o_ev, l, NTILE)
                stand(pe)
                def three(out_, w_hi, w_lo, x_hi, x_lo, first, last):
                    for h in range(2):
                        c = slice(h * HALF, (h + 1) * HALF)
                        mm(out_[h], w_hi, x_hi[:, c], start=first, stop=False, skip_group_check=True)
                        mm(out_[h], w_hi, x_lo[:, c], start=False, stop=False, skip_group_check=True)
                        ins = mm(out_[h], w_lo, x_hi[:, c], start=False, stop=last, skip_group_check=True)
                    return ins

                with pe.Fori(0, 4) as dp:
                    for v in range(6):
                        q, s = 4 * (v % 2), v % 2
                        k0, k1 = BR_K[v % 3]
                        pe.wait_ge(br_pr[0], l * 24 + dp * 6 + (v - 1 + br_pr[2]))
                        pe.wait_ge(g_lo[0], l * g_lo[1] + dp * 6 + (v + 1 + g_lo[2]))
                        for k in range(DC):
                            if v == 0 and k >= 3:
                                wait(pe, sp_lo, l, k + 5)
                            three([bank(q, HALF), bank(q + 1, HALF)], gate_hi[s][:, k, :], gate_lo[s][:, k, :], xn_hi[k], xn_lo[:, k, :],
                                  k == 0, k == DC - 1)
                        pe.wait_ge(b_lo[0], l * b_lo[1] + dp * 6 + (v + 1 + b_lo[2]))
                        for k in range(k0, k1):
                            if v == 1:
                                wait(pe, sp_lo, l, k + 11)
                            ins = three([bank(q + 2, HALF), bank(q + 3, HALF)], brw_hi[s][:, k - k0, :], brw_lo[s][:, k - k0, :],
                                        ybr_hi[k], ybr_lo[:, k, :], k == k0, k == k1 - 1)
                        ins.then_inc(br_mm[0], 1)

                wait(pe, br_pr, l, 24)
                for dt in range(DC):
                    wait(pe, g_lo, l, 24 + dt + 1)
                    if dt >= 4:
                        wait(pe, x_mid, l, dt - 3)
                    b = 2 * (dt % 4)
                    for k in range(DC):
                        if dt == 0:
                            wait(pe, h_lo, l, k + 1)
                        ins = three([bank(b, HALF), bank(b + 1, HALF)], gate_hi[dt % 2][:, k, :], gate_lo[dt % 2][:, k, :],
                                    hT_hi[:, k, :], hT_lo[:, k, :], k == 0, k == DC - 1)
                    ins.then_inc(wo_mm[0], 1)

                norm(1)
                for k in range(DC):
                    wait(pe, xn_rdy, l, DC + k + 1)
                    if k == 0:
                        stand(pe)
                    for h in range(2):
                        ins = mm(ps[0:20, h, 0:HALF], wrt[:, k, :], xn[:, k, h * HALF:(h + 1) * HALF],
                                 start=(k == 0), stop=(k == DC - 1), skip_group_check=True)
                ins.then_inc(rt_mm[0], 1)
                for t in range(NTILE):
                    if t >= 3:
                        wait(pe, xt_ev, l, t - 2)
                    for k in range(DC):
                        ins = nc.tensor.transpose(bank(2 + 2 * (t % 3) + k // 4, P, TM[t], P * (k % 4)), xn[:, k, TO[t]:TO[t] + TM[t]], ident)
                    ins.then_inc(xt_mm[0], 1)
                    if t == 0:
                        wait(pe, lg_ev, l, 1)
                        stand(pe)
                        for i in range(NTILE):
                            ins = nc.tensor.transpose(ps[0:TM[i], 0, 20 * i:20 * i + 20], logitT[:, TO[i]:TO[i] + TM[i]], ident[0:20, 0:20])
                        ins.then_inc(lg_tr[0], 1)
                wait(pe, oh_rdy, l, 1)
                cnt = ps[:, 1, 0:96]
                mm(cnt, stri, oh_both, start=True, stop=False, skip_group_check=True)
                for j in range(NTILE):
                    n = NTILE - j
                    ins = mm(cnt[:, 16 * (j + 1):].rearrange("p (t e) -> p t e", t=n), ones[:, :],
                             oh_both[:, 16 * j:16 * j + 16].unsqueeze(1).to_broadcast([P, n, NE]),
                             start=False, stop=(j == NTILE - 1), skip_group_check=True)
                ins.then_inc(rk_mm[0], 1)

                def turn_rows(s, n):
                    for k in range(DC):
                        ins = nc.tensor.transpose(bank(k // 4, P, P, P * (k % 4)), xg[:, s, k * P:(k + 1) * P], ident)
                    ins.then_inc(xg_tr[0], 1)

                def turn_act(s, n):
                    pe.wait_ge(eh_h[0], n)
                    for k in range(2):
                        ins = nc.tensor.transpose(bank(2 + s, P, P, P * k), hh[:, s, P * k:P * k + P], ident)
                    ins.then_inc(eh_tr[0], 1)

                pairs = pairs_in_use(pe, l)
                wait(pe, xt_ev, l, NTILE)
                for s in range(2):
                    pe.wait_ge(xg_in[s][0], l * (NR * 8) + 16)
                    if s:
                        pe.wait_ge(xg_ev[0], l * NR + 1)
                    turn_rows(s, 0)
                with pe.Fori(0, NT // 2) as it:
                    with pe.If(it < pairs):
                        for s in range(2):
                            pe.wait_ge(gu_in[s][0], l * (NT * 16) + it * 32 + 32)
                            pe.wait_ge(xg_ev[0], l * NR + it * 2 + (s + 1))
                            g = guw[s].rearrange("p (k m n) -> p k m n", k=DC, m=2)
                            for m in range(2):
                                for k in range(DC):
                                    ins = mm(bank(2 + s, 256, P, 256 * m), xgT[:, s, k, :], g[:, k, m, :], start=(k == 0), stop=(k == DC - 1), skip_group_check=True)
                            ins.then_inc(gu_mm[0], 1)
                        for s in range(2):
                            n = l * NT + it * 2 + (s + 1)
                            turn_act(s, n)
                            pe.wait_ge(xg_in[s][0], l * (NR * 8) + it * 16 + 32)
                            pe.wait_ge(xg_ev[0], l * NR + it * 2 + (s + 2))
                            turn_rows(s, n)
                            pe.wait_ge(dn_in[s][0], l * (NT * 16) + it * 32 + 32)
                            pe.wait_ge(eh_ev[0], n)
                            pe.wait_ge(yo_ev[0], l * NT + it * 2 + (s - 1 + yo_ev[2]))
                            d = down_w[s].rearrange("p (k a) n -> p k a n", k=2)
                            for a in range(2):
                                for k in range(2):
                                    ins = mm(bank(4 + 2 * s + a), ehT[:, s, P * k:P * k + P], d[:, k, a, :], start=(k == 0), stop=(k == 1))
                            ins.then_inc(dn_mm[0], 1)
                    with pe.Else():
                        pass_pair(pe, l, it, (gu_mm, 2), (xg_tr, 2), (eh_tr, 2), (dn_mm, 2))

                for t in range(NTILE):
                    wait(pe, cb_2, l, t + 1)
                    if t == 4:
                        wait(pe, x_in, l, NTILE + 1)
                    stand(pe)
                    for k in range(DC):
                        ins = nc.tensor.transpose(bank(2 * (t % 4) + k // 4, TM[t], P, P * (k % 4)), g1[0:TM[t], t, k * P:(k + 1) * P], ident[0:TM[t], 0:TM[t]])
                    ins.then_inc(cb_tr[0], 1)

            pe.wait_ge(x_in[0], NTILE * (DEPTH + 1))
            for t in range(NTILE):
                if t >= 2:
                    pe.wait_ge(y_ev[0], t - 1)
                for k in range(DC):
                    ins = nc.tensor.transpose(bank(2 * (t % 2) + k // 4, P, TM[t], P * (k % 4)), xT[:, k, TO[t]:TO[t] + TM[t]], ident)
                ins.then_inc(y_tr[0], 1)

        @block.scalar
        def _(act):
            f = nc.scalar.activation
            starts(act, ys_wr, yo_ev, cb_1)
            act.wait_ge(dve_fills[0], DVE_FILLS)

            def banks(b, m=P):
                return ps[0:m, b:b + 2, 0:HALF]

            def halves(ap):
                return ap.rearrange("p (h n) -> p h n", h=2)

            with act.Fori(0, DEPTH) as l:
                def square(k):
                    f(xn[:, k, :], xT[:, k, :], ACT.Square).then_inc(norm_sq[0], 1)

                def rstd(w):
                    wait(act, norm_mm, l, w + 1)
                    f(halves(rs[:, :]), banks((6, 0)[w]), ACT.Ln, bias=eps, scale=1.0 / D).then_inc(norm_ln[0], 1)
                    wait(act, norm_ln, l, w + 1)
                    f(rs[:, :], rs[:, :], ACT.Exp, scale=-0.5).then_inc(norm_rs[0], 1)

                act.preload_act_table_set(TABLE_LN_EXP)
                wait(act, outs, l, 0)
                wait(act, x_in, l, NTILE)
                for k in range(DC):
                    square(k)
                rstd(0)
                for c in range(4):
                    for t in range(NTILE):
                        g, m = c * NTILE + t, TM[t]
                        wait(act, tk_mm, l, g + 1)
                        n = (256, 160, 256, 256)[c]
                        if c < 2:
                            w = (Q_LORA, KV_LORA)[c]
                            f(work[0:m, 256 * g:256 * g + w], ps[0:m, g % 6, 0:w], ACT.Square, accum_out=lss[0:m, 5 * c + t:5 * c + t + 1]).then_inc(lss_rdy[0], 1)
                        dst = (toka[0:m, t, 0:256], toka[0:m, t, 256:416], ksv[0:m, t, 0:256], ksv[0:m, t, 256:512])[c]
                        f(dst, ps[0:m, g % 6, 0:n], ACT.Copy).then_inc(tk_ev[0], 1)
                    if c == 1:
                        wait(act, lss_rdy, l, 10)
                        f(lrs[:, 0:5], lss[:, 0:5], ACT.Ln, bias=eps, scale=1.0 / Q_LORA).then_inc(lrs_ln[0], 1)
                        f(lrs[:, 5:10], lss[:, 5:10], ACT.Ln, bias=eps, scale=1.0 / KV_LORA).then_inc(lrs_ln[0], 1)
                        wait(act, lrs_ln, l, 2)
                        f(lrs[:, :], lrs[:, :], ACT.Exp, scale=-0.5).then_inc(lrs_rdy[0], 1)
                for m in range(2):
                    wait(act, cm_mm, l, m + 1)
                    f(halves(qs[:, m, :]), banks(2 * m), ACT.Copy, scale=0.125).then_inc(qs_ev[0], 1)
                for m in range(2):
                    wait(act, cm_mm, l, m + 3)
                    b = (4, 6)[m]
                    f(u[:, m, UP:UP + HALF], ps[:, b, 0:HALF], ACT.Copy).then_inc(u_ev[0], 1)
                    f(u[:, m, UP + HALF:UP + SEQ], ps[:, b + 1, 0:SEQ - HALF], ACT.Copy).then_inc(u_ev[0], 1)
                    f(u[:, m, US:US + DEC], ps[:, b + 1, SEQ - HALF:HALF], ACT.Copy).then_inc(u_ev[0], 1)
                wait(act, smalls, l, 320)
                g = 0
                for dst, scale in ([(kst[:, m], None) for m in range(2)] + [(lT[:, :], None)]
                                   + [(cqT[:, m], gains[:, G_QL + m:G_QL + m + 1]) for m in range(2)]):
                    for lo, hi in ((0, SEQ), (SEQ, T if scale is not None else KEYS)):
                        wait(act, tp_mm, l, g + 1)
                        kw_ = {} if scale is None else {"scale": scale}
                        f(dst[:, lo:hi], ps[:, g % 6, 0:hi - lo], ACT.Copy, **kw_).then_inc(tp_ev[0], 1)
                        g += 1
                wait(act, po_tr, l, 1)
                f(pool_out[:, :], ps[0:16, 7, :], ACT.Copy).then_inc(po_ev[0], 1)
                wait(act, spill, l, 16)
                for m in range(2):
                    wait(act, pl_mm, l, m + 1)
                    f(halves(ybr[:, m, :]), banks(2 * m), ACT.Copy, scale=gains[:, G_PS + m:G_PS + m + 1]).then_inc(pl_ev[0], 1)

                def kq_rstd(n):
                    m = KM[n] if n < 7 else TM[n - 7]
                    wait(act, kq_ss, l, n + 1)
                    f(kss[0:m, n % 2], kss[0:m, n % 2], ACT.Ln, bias=eps[0:m], scale=1.0 / QK).then_inc(kq_ln[0], 1)
                    wait(act, kq_ln, l, n + 1)
                    f(kss[0:m, n % 2], kss[0:m, n % 2], ACT.Exp, scale=-0.5).then_inc(kq_rs[0], 1)

                for n in range(12):
                    m = KM[n] if n < 7 else TM[n - 7]
                    b = 2 * (n % 2)
                    wait(act, kq_mm, l, n + 1)
                    if n >= 3:
                        wait(act, kq_tp, l, n - 2)
                    if n < 7:
                        f(kw[0:m, n % 3, :].rearrange("p (h n) -> p h n", h=HEADS)[:, :, 0:NOPE],
                          ps[0:m, b:b + 2, :].rearrange("p b (h n) -> p (b h) n", h=4)[:, :, 0:NOPE], ACT.Copy).then_inc(kq_cp[0], 1)
                    else:
                        f(kw[0:m, n % 3, :].rearrange("p (b n) -> p b n", b=2), ps[0:m, b:b + 2, 0:384], ACT.Copy).then_inc(kq_cp[0], 1)
                    if n:
                        kq_rstd(n - 1)
                    wait(act, kq_raw, l, n + 1)
                    f(sq[0:m, n % 2, :], kw[0:m, n % 3, :], ACT.Square).then_inc(kq_sq[0], 1)
                kq_rstd(11)

                zf = ps[:, :, :].rearrange("p b n -> p (b n)")

                def softplus_tail(h):
                    z = zf[:, 1536 * (h % 2):1536 * (h % 2) + SBC]
                    wait(act, z_mm, l, h + 1)
                    if h:
                        wait(act, sp_raw, l, h)
                    f(zs, z, ACT.Abs).then_inc(z_abs[0], 1)
                    wait(act, z_abs, l, h + 1)
                    f(zs, zs, ACT.Exp, scale=-1.0).then_inc(z_exp[0], 1)
                    wait(act, z_exp, l, h + 1)
                    f(zs, zs, ACT.Ln, bias=1.0).then_inc(z_ln[0], 1)

                def high(j):
                    src, dst, _ = SPLITS[j]
                    f(dst, src, ACT.Copy).then_inc(sp_hi[0], 1)

                def gate_high(s, slot, lo):
                    src = wr[:, slot, :].rearrange("p (k n) -> p k n", k=DC)[:, :, lo:lo + P]
                    f(gate_hi[s], src, ACT.Copy).then_inc(g_hi[0], 1)

                softplus_tail(0)
                softplus_tail(1)
                wait(act, pl_ev, l, 2)
                for j in range(3):
                    high(j)
                for h in range(SBH):
                    wait(act, sfx_mm, l, h + 1)
                    if h >= 2:
                        wait(act, sv_mm, l, h - 1)
                    f(aa[:, h % 2], zf[:, 1536 * (h % 2):1536 * (h % 2) + SBC], ACT.Exp).then_inc(a_raw[0], 1)
                    if h + 2 < SBH:
                        softplus_tail(h + 2)
                    if h % 2:
                        wait(act, sv_mm, l, h + 1)
                        f(ybr[:, 6 + h // 2, 0:SEQ], ps[:, 6, :], ACT.Copy).then_inc(sv_ev[0], 1)
                        f(ybr[:, 6 + h // 2, SEQ:T], ps[:, 7, 0:DEC], ACT.Copy).then_inc(sv_ev[0], 1)

                def out_rows(t):
                    wait(act, o_tr, l, t + 1)
                    f(ybr[:, 2:6, TO[t]:TO[t] + TM[t]], ps[:, 7, :].rearrange("p (k n) -> p k n", k=4)[:, :, 0:TM[t]], ACT.Copy).then_inc(o_ev[0], 1)

                for n in range(NU):
                    t, h = n // HEADS, n % HEADS
                    m, nk = TM[t], (P * (t + 1) if t < 4 else 288)
                    wait(act, s_max, l, n + 1)
                    if n >= 3:
                        wait(act, pt_mm, l, n - 2)
                    f(pr[0:m, n % 3, 0:nk], ps[0:m, n % 3, 0:nk], ACT.Exp, bias=nmax[0:m, n % 3:n % 3 + 1],
                      accum_out=sums[0:m, t, h:h + 1]).then_inc(s_exp[0], 1)
                    if n % HEADS == 3 and n > HEADS:
                        out_rows(t - 1)
                    if n == 5:
                        wait(act, sv_ev, l, 4)
                    if n in (5, 10, 14, 18, 22):
                        high(3 + (5, 10, 14, 18, 22).index(n))
                    if n == 26:
                        wait(act, w_in_[0], l, 96)
                        wait(act, outs, l, 160)
                        gate_high(0, 0, 0)
                out_rows(NTILE - 1)
                for j in range(8, 16):
                    if j == 12:
                        wait(act, o_ev, l, NTILE)
                    high(j)

                act.preload_act_table_set(TABLE_SIGMOID)
                with act.Fori(0, 4) as dp:
                    for v in range(6):
                        k0, k1 = BR_K[v % 3]
                        if v < 3:
                            act.wait_ge(wbr_in[v][0], l * wbr_in[v][1] + dp * 16 + 16)
                        act.wait_ge(br_mm[0], l * 24 + dp * 6 + (v - 1 + br_mm[2]))
                        f(brw_hi[v % 2][:, 0:k1 - k0, :], wr[:, 3, :].rearrange("p (k n) -> p k n", k=DC)[:, k0:k1, P * (v // 3):P * (v // 3) + P],
                          ACT.Copy).then_inc(b_hi[0], 1)
                        w = (v + 1) % 6
                        if w < 3:
                            act.wait_ge(w_in_[w][0], l * w_in_[w][1] + dp * 32 + (96 + 32 * (v // 5)))
                        act.wait_ge(br_mm[0], l * 24 + dp * 6 + (v + br_mm[2]))
                        gate_high((v + 1) % 2, w % 3, P * (w // 3))
                        act.wait_ge(br_mm[0], l * 24 + dp * 6 + (v + 1 + br_mm[2]))
                        f(halves(sg[:, v % 2, :]), banks(4 * (v % 2)), ACT.Sigmoid).then_inc(br_sg[0], 1)
                        if v % 3 == 2:
                            act.wait_ge(h_sum[0], l * DC + dp * 2 + (v // 3 + 1))
                            f(hT_hi[:, bass.ds(dp * 2 + v // 3, 1), :].rearrange("p o n -> p (o n)"), hsum, ACT.Copy).then_inc(h_hi[0], 1)

                act.preload_act_table_set(TABLE_LN_EXP)
                for dt in range(DC):
                    if dt < DC - 1:
                        if dt % 2:
                            c = (dt + 1) // 2
                            wait(act, w_in_[c], l, w_in_[c][1])
                        if dt == 0:
                            wait(act, br_mm, l, 24)
                        else:
                            wait(act, wo_mm, l, dt)
                        gate_high((dt + 1) % 2, (dt + 1) // 2, P * ((dt + 1) % 2))
                    if dt >= 2:
                        wait(act, x_mid, l, dt - 1)
                        square(dt - 2)
                for k in range(DC - 2, DC):
                    wait(act, x_mid, l, k + 1)
                    square(k)
                rstd(1)
                wait(act, rt_mm, l, 1)
                f(halves(logitT), ps[0:20, 0:2, 0:HALF], ACT.Copy).then_inc(lg_ev[0], 1)
                for t in range(NTILE):
                    wait(act, xt_mm, l, t + 1)
                    b = 2 + 2 * (t % 3)
                    f(xtok[0:TM[t], t, :].rearrange("p (b n) -> p b n", b=2), ps[0:TM[t], b:b + 2, :], ACT.Copy).then_inc(xt_ev[0], 1)
                wait(act, rt_e, l, 1)
                f(r_eg, r_eg, ACT.Exp).then_inc(rt_x[0], 1)
                wait(act, rt_e, l, 2)
                f(r_e2, r_e2, ACT.Exp).then_inc(rt_x[0], 1)

                act.preload_act_table_set(TABLE_SIGMOID)
                pairs = pairs_in_use(act, l)
                with act.Fori(0, NT // 2) as it:
                    with act.If(it < pairs):
                        for s in range(2):
                            act.wait_ge(gu_mm[0], l * NT + it * 2 + (s + 1 + gu_mm[2]))
                            f(hh[:, s], ps[:, 2 + s, 0:DE], ACT.Sigmoid).then_inc(eh_sg[0], 1)
                        for s in range(2):
                            act.wait_ge(dn_mm[0], l * NT + it * 2 + (s + 1 + dn_mm[2]))
                            act.wait_ge(ys_wr[0], pair_done(l, it) + 16 * s)
                            f(yo.rearrange("p (b n) -> p b n", b=2), ps[:, 4 + 2 * s:6 + 2 * s, :], ACT.Copy).then_inc(yo_ev[0], 1)
                            act.wait_ge(yo_ev[0], l * NT + it * 2 + (s + 1 + yo_ev[2]))
                            act.dma_start(row_tiles[bass.ds(it * 2 + s, 1)].rearrange("o p n -> p (o n)"),
                                          yo).then_inc(ys_wr[0], 16)
                    with act.Else():
                        pass_pair(act, l, it, (eh_sg, 2), (yo_ev, 2), (ys_wr, 32))
                for t in range(NTILE):
                    g = g1[0:TM[t], t, :]
                    wait(act, gath[t], l, 32)
                    f(g, g, ACT.Copy, scale=r_w1[0:TM[t], t:t + 1]).then_inc(cb_1[0], 1)

        @block.vector
        def _(dve):
            v_ = nc.vector
            starts(dve, br_pr, g_lo, b_lo)
            nfill = 0

            def fill(ap, val):
                nonlocal nfill
                nfill += 1
                v_.memset(ap, val).then_inc(dve_fills[0], 1)

            fill(ones[:, :], 1.0)
            fill(nones[:, :], -1.0)
            fill(negrow[:, :], NEG)
            fill(small[:, :], 1.0)
            fill(hist[0:1, :], 0.0)
            fill(wpl[:, :, :], 0.0)
            fill(rt[:, :], 0.0)
            fill(ints[:, :], 0)
            fill(kst[:, :, :], 0.0)
            dve.wait_ge(dve_fills[0], nfill)
            fill(eps, EPS)
            assert nfill == DVE_FILLS, nfill
            for t in range(NTILE):
                dve.wait_ge(x_tr[0], t + 1)
                b = 2 * (t % 4)
                v_.tensor_copy(xT[:, :, TO[t]:TO[t] + TM[t]].rearrange("p (b k) n -> p b k n", b=2),
                               ps[:, b:b + 2, :].rearrange("p b (k n) -> p b k n", k=4)[:, :, :, 0:TM[t]]).then_inc(x_in[0], 1)

            v_.memset(toka[:, 4, :], 0.0).then_inc(x_tr[0], 1)

            with dve.Fori(0, DEPTH) as l:
                links = 0

                def link(ins):
                    nonlocal links
                    links += 1
                    ins.then_inc(dve_link[0], 1)
                    wait(dve, dve_link, l, links)

                def tt(o_, a, b, op):
                    return v_.tensor_tensor(o_, a, b, op)

                def norm(w):
                    if w == 0:
                        wait(dve, smalls, l, 320)
                    wait(dve, norm_rs, l, w + 1)
                    for k in range(DC):
                        v_.scalar_tensor_tensor(out=xn[:, k, :], in0=xT[:, k, :], scalar=gains[:, 8 * w + k:8 * w + k + 1],
                                                in1=rs[:, :], op0=ALU.mult, op1=ALU.mult).then_inc(xn_rdy[0], 1)

                wait(dve, outs, l, 0)
                norm(0)
                v_.tensor_scalar(gains[0:QK, G_Q:G_Q + 1], gains[0:QK, G_Q:G_Q + 1], QK ** -0.5, None, ALU.mult).then_inc(gpre[0], 1)
                v_.memset(u[:, :, 0:16], 0.0).then_inc(hz[0], 1)
                wait(dve, lrs_rdy, l, 1)
                for t in range(NTILE):
                    m = TM[t]
                    v_.tensor_scalar(toka[0:m, t, 0:256], toka[0:m, t, 0:256], lrs[0:m, t:t + 1], None, ALU.mult).then_inc(cq_n[0], 1)
                    v_.scalar_tensor_tensor(out=lat[0:m, t, :], in0=toka[0:m, t, 256:384], scalar=lrs[0:m, 5 + t:6 + t],
                                            in1=gk_bc[0:m, :], op0=ALU.mult, op1=ALU.mult).then_inc(lat_n[0], 1)
                x1, x2 = toka[:, :, 384:400], toka[:, :, 400:416]
                rk = rope_t[:, :, 0:80].rearrange("p a (t n) -> p a t n", t=5)
                tt(rk[:, 0], x1, cos, ALU.mult)
                tt(rk[:, 1], x2, sin, ALU.mult)
                tt(rk[:, 2], x1, sin, ALU.mult)
                link(tt(rk[:, 3], x2, cos, ALU.mult))
                tt(krt[:, 0:5, 0:HR], rk[:, 0], rk[:, 1], ALU.subtract)
                tt(krt[:, 0:5, HR:ROPE], rk[:, 2], rk[:, 3], ALU.add).then_inc(kr_n[0], 1)

                wait(dve, h_tr, l, 1)
                v_.tensor_copy(u[:, :, US - 16:US], ps[:, 7, 0:32].rearrange("p (m n) -> p m n", m=2)).then_inc(h_ev[0], 1)
                wait(dve, u_ev, l, 6)
                wait(dve, h_ev, l, 1)
                wait(dve, hz, l, 1)
                N = UW
                link(tt(sa[:, :, 1:N], u[:, :, 1:N], u[:, :, 0:N - 1], ALU.add))
                tt(sb_[64:128, 0, 3:N], sa[64:128, 0, 3:N], sa[64:128, 0, 1:N - 2], ALU.add)
                link(tt(sb_[:, 1, 3:N], sa[:, 1, 3:N], sa[:, 1, 1:N - 2], ALU.add))
                link(tt(sa[:, 1, 7:N], sb_[:, 1, 7:N], sb_[:, 1, 3:N - 4], ALU.add))
                link(tt(sb_[64:128, 1, 15:N], sa[64:128, 1, 15:N], sa[64:128, 1, 7:N - 8], ALU.add))
                for g, w in enumerate(WINDOWS):
                    q, m, s_ = 64 * (g % 2), g // 2, (sa, sb_)[g % 2]
                    for lo, n, dst in ((UP + 16, SEQ - 16, 16), (US, DEC, SEQ)):
                        v_.scalar_tensor_tensor(out=yp[q:q + 64, m, dst:dst + n], in0=s_[q:q + 64, m, lo:lo + n], scalar=1.0 / w,
                                                in1=u[q:q + 64, m, lo:lo + n], op0=ALU.mult, op1=ALU.subtract)
                    tt(yp[q:q + 64, m, 0:16], s_[q:q + 64, m, UP:UP + 16], invc[q:q + 64, m, :], ALU.mult)
                link(v_.memset(small[:, 44:45], 0.0))
                tt(yp[:, :, 0:16], yp[:, :, 0:16], u[:, :, UP:UP + 16], ALU.subtract).then_inc(yp_rdy[0], 1)

                def kq_evac(n):
                    wait(dve, kq_tp, l, n + 1)
                    if n < 7:
                        dst, m, gain = kT[0:QK, :, KO[n]:KO[n] + KM[n]], KM[n], gains[0:QK, G_K:G_K + 1]
                    else:
                        dst, m, gain = qT[0:QK, :, TO[n - 7]:TO[n - 7] + TM[n - 7]], TM[n - 7], gains[0:QK, G_Q:G_Q + 1]
                    b = 4 + 2 * (n % 2)
                    v_.tensor_scalar(dst.rearrange("p (b h) n -> p b h n", b=2),
                                     ps[0:QK, b:b + 2, :].rearrange("p b (h n) -> p b h n", h=4)[:, :, :, 0:m], gain, None, ALU.mult).then_inc(kq_ev[0], 1)

                def kq_scale(n):
                    m = KM[n] if n < 7 else TM[n - 7]
                    k3 = kw[0:m, n % 3, :].rearrange("p (h n) -> p h n", h=HEADS)
                    wait(dve, kq_rs, l, n + 1)
                    tt(k3, k3, kss[0:m, n % 2].unsqueeze(2).to_broadcast([m, HEADS, QK]), ALU.mult).then_inc(kq_n[0], 1)

                wait(dve, gpre, l, 1)
                wait(dve, kr_n, l, 1)
                wait(dve, po_tr, l, 1)
                wait(dve, tp_mm, l, 10)
                for n in range(12):
                    wait(dve, kq_cp, l, n + 1)
                    b = 2 * (n % 2)
                    k3 = kw[:, n % 3, :].rearrange("p (h n) -> p h n", h=HEADS)
                    if n < 7:
                        m = KM[n]
                        v_.tensor_copy(vv[0:m, n, :].rearrange("p (h n) -> p h n", h=HEADS),
                                       ps[0:m, b:b + 2, :].rearrange("p b (h n) -> p (b h) n", h=4)[:, :, NOPE:P])
                        v_.tensor_copy(k3[0:m, :, NOPE:QK], krt[0:m, n, :].unsqueeze(1).to_broadcast([m, HEADS, ROPE])).then_inc(kq_raw[0], 1)
                    else:
                        t, m = n - 7, TM[n - 7]
                        x1, x2 = k3[0:m, :, NOPE:NOPE + HR], k3[0:m, :, NOPE + HR:QK]
                        c_ = cos[0:m, t, :].unsqueeze(1).to_broadcast([m, HEADS, HR])
                        s_ = sin[0:m, t, :].unsqueeze(1).to_broadcast([m, HEADS, HR])
                        r = rope_t[0:m, :, :].rearrange("p a (h n) -> p a h n", h=HEADS)
                        tt(r[:, 0], x1, c_, ALU.mult)
                        tt(r[:, 1], x2, s_, ALU.mult)
                        tt(r[:, 2], x1, s_, ALU.mult)
                        link(tt(r[:, 3], x2, c_, ALU.mult))
                        tt(x1, r[:, 0], r[:, 1], ALU.subtract)
                        tt(x2, r[:, 2], r[:, 3], ALU.add).then_inc(kq_raw[0], 1)
                    if n:
                        kq_scale(n - 1)
                    if n >= 2:
                        kq_evac(n - 2)
                    wait(dve, kq_sq, l, n + 1)
                    v_.tensor_reduce(kss[0:m, n % 2], sq[0:m, n % 2, :].rearrange("p (h n) -> p h n", h=HEADS), AX, ALU.add).then_inc(kq_ss[0], 1)
                kq_scale(11)
                kq_evac(10)
                kq_evac(11)

                def low(j):
                    src, hi, lo = SPLITS[j]
                    wait(dve, sp_hi, l, j + 1)
                    tt(lo, src, f32(hi), ALU.subtract).then_inc(sp_lo[0], 1)

                def gate_low(s, slot, lo):
                    src = wr[:, slot, :].rearrange("p (k n) -> p k n", k=DC)[:, :, lo:lo + P]
                    tt(gate_lo[s], src, f32(gate_hi[s]), ALU.subtract).then_inc(g_lo[0], 1)

                zf = ps[:, :, :].rearrange("p b n -> p (b n)")
                for h in range(SBH):
                    wait(dve, z_ln, l, h + 1)
                    if h:
                        wait(dve, sfx_mm, l, h)
                    v_.scalar_tensor_tensor(out=sp_, in0=zf[:, 1536 * (h % 2):1536 * (h % 2) + SBC], scalar=0.0, in1=zs,
                                            op0=ALU.max, op1=ALU.add).then_inc(sp_raw[0], 1)
                    if 1 <= h < 4:
                        low(h - 1)

                def neg_max(n):
                    t = n // HEADS
                    m, nk = TM[t], (P * (t + 1) if t < 4 else 288)
                    wait(dve, s_mm, l, n + 1)
                    if n >= 3:
                        wait(dve, s_exp, l, n - 2)
                    v_.tensor_reduce(nmax[0:m, n % 3:n % 3 + 1], ps[0:m, n % 3, 0:nk], AX, ALU.max, negate=True).then_inc(s_max[0], 1)

                def normalise(t):
                    m = TM[t]
                    wait(dve, pv_mm, l, HEADS * (t + 1))
                    link(v_.reciprocal(sums[0:m, t, :], sums[0:m, t, :]))
                    if t:
                        wait(dve, o_tr, l, t)
                    tt(ot[0:m, :].rearrange("p (h n) -> p h n", h=HEADS), ps[0:m, 5 + t % 2, :].rearrange("p (h n) -> p h n", h=HEADS),
                       sums[0:m, t, :].unsqueeze(2).to_broadcast([m, HEADS, VD]), ALU.mult).then_inc(o_nrm[0], 1)

                neg_max(0)
                neg_max(1)
                for n in range(NU):
                    t = n // HEADS
                    if n + 2 < NU:
                        neg_max(n + 2)
                    wait(dve, pt_mm, l, n + 1)
                    if n >= 2:
                        wait(dve, pv_mm, l, n - 1)
                    if t < 4:
                        v_.tensor_copy(pt[:, n % 2, 0:P * (t + 1)], ps[:, 3 + n % 2, 0:P * (t + 1)]).then_inc(pt_ev[0], 1)
                    else:
                        v_.tensor_copy(pt[:, n % 2, DEC:3 * DEC], ps[:, 3 + n % 2, DEC:3 * DEC])
                        v_.tensor_copy(pt[0:DEC, n % 2, 0:DEC], ps[0:DEC, 3 + n % 2, 0:DEC]).then_inc(pt_ev[0], 1)
                    if n % HEADS == 1 and n > HEADS:
                        normalise(t - 1)
                    if n in (5, 10, 14, 18, 22):
                        low(3 + (5, 10, 14, 18, 22).index(n))
                    if n == 26:
                        wait(dve, g_hi, l, 1)
                        gate_low(0, 0, 0)
                normalise(NTILE - 1)
                for j in range(8, 16):
                    low(j)

                def halves(ap):
                    return ap.rearrange("p (h n) -> p h n", h=2)

                with dve.Fori(0, 4) as dp:
                    for v in range(6):
                        b = v % 3
                        q = 4 * (v % 2) + 2
                        k0, k1 = BR_K[b]
                        dve.wait_ge(b_hi[0], l * 24 + dp * 6 + (v + 1))
                        tt(brw_lo[v % 2][:, 0:k1 - k0, :], wr[:, 3, :].rearrange("p (k n) -> p k n", k=DC)[:, k0:k1, P * (v // 3):P * (v // 3) + P],
                           f32(brw_hi[v % 2][:, 0:k1 - k0, :]), ALU.subtract).then_inc(b_lo[0], 1)
                        w = (v + 1) % 6
                        dve.wait_ge(g_hi[0], l * 32 + dp * 6 + (v + 2))
                        gate_low((v + 1) % 2, w % 3, P * (w // 3))
                        dve.wait_ge(br_sg[0], l * 24 + dp * 6 + (v + 1))
                        if b == 2:
                            dve.wait_ge(br_ac[0], l * 8 + dp * 2 + (v // 3 + 1))
                        tt(halves(acc if b == 0 else tmp), halves(sg[:, v % 2, :]), ps[:, q:q + 2, 0:HALF], ALU.mult).then_inc(br_pr[0], 1)
                        if b:
                            dve.wait_ge(br_pr[0], l * 24 + dp * 6 + (v + 1 + br_pr[2]))
                        if b == 1:
                            tt(acc, acc, tmp, ALU.add).then_inc(br_ac[0], 1)
                        if b == 2:
                            tt(hsum, acc, tmp, ALU.add).then_inc(h_sum[0], 1)
                            dve.wait_ge(h_hi[0], l * DC + dp * 2 + (v // 3 + 1))
                            dt = bass.ds(dp * 2 + v // 3, 1)
                            tt(hT_lo[:, dt, :].rearrange("p o n -> p (o n)"), hsum, f32(hT_hi[:, dt, :].rearrange("p o n -> p (o n)")),
                               ALU.subtract).then_inc(h_lo[0], 1)

                wait(dve, reload_, l, 16)
                for dt in range(DC):
                    if dt < DC - 1:
                        wait(dve, g_hi, l, 24 + dt + 2)
                        gate_low((dt + 1) % 2, (dt + 1) // 2, P * ((dt + 1) % 2))
                    wait(dve, wo_mm, l, dt + 1)
                    b = 2 * (dt % 4)
                    tt(halves(xT[:, dt, :]), halves(xT[:, dt, :]), ps[:, b:b + 2, 0:HALF], ALU.add).then_inc(x_mid[0], 1)
                norm(1)

                def first(dst, x, mx, n_groups):
                    link(tt(dst, x, mx.unsqueeze(2).to_broadcast([P, NTILE, 4]), ALU.is_equal))
                    link(tt(r_v, dst, j_less, ALU.mult))
                    link(v_.tensor_reduce(r_f, r_v, AX, ALU.min))
                    link(tt(dst, j_less, r_f.unsqueeze(2).to_broadcast([P, NTILE, 4]), ALU.is_equal))

                wait(dve, lg_tr, l, 1)
                link(tt(r_lg, ps[:, 0, 0:100].rearrange("p (t n) -> p t n", t=NTILE),
                        bias_bc[:, :].unsqueeze(1).to_broadcast([P, NTILE, 20]), ALU.add))
                link(v_.tensor_reduce(r_m, r_lg[:, :, 0:4], AX, ALU.max))
                first(r_og, r_lg[:, :, 0:4], r_m, 1)
                tt(r_eg, r_lg[:, :, 0:4], r_m.unsqueeze(2).to_broadcast([P, NTILE, 4]), ALU.subtract).then_inc(rt_e[0], 1)
                link(tt(r_t16, r_lg[:, :, 4:20].rearrange("p t (g e) -> p t g e", g=NG),
                        r_og.unsqueeze(3).to_broadcast([P, NTILE, NG, EPG]), ALU.mult))
                link(v_.tensor_reduce(r_le, r_t16.rearrange("p t g e -> p t e g"), AX, ALU.add))
                link(v_.tensor_reduce(r_m1, r_le, AX, ALU.max))
                first(r_o1, r_le, r_m1, 1)
                link(v_.scalar_tensor_tensor(out=r_l2, in0=r_o1, scalar=NEG, in1=r_le, op0=ALU.mult, op1=ALU.add))
                link(v_.tensor_reduce(r_m2, r_l2, AX, ALU.max))
                first(r_o2, r_l2, r_m2, 1)
                tt(r_e2, r_m2, r_m1, ALU.subtract).then_inc(rt_e[0], 1)
                link(tt(r_og, r_og, valid, ALU.mult))
                for w, oh in enumerate((r_o1, r_o2)):
                    tt(oh12[:, w].rearrange("p (t g e) -> p t g e", t=NTILE, g=NG), r_og.unsqueeze(3).to_broadcast([P, NTILE, NG, EPG]),
                       oh.unsqueeze(2).to_broadcast([P, NTILE, NG, EPG]), ALU.mult)
                link(v_.memset(small[:, 44:45], 0.0))
                tt(oh_both[:, 0:80], oh12[:, 0], oh12[:, 1], ALU.add).then_inc(oh_rdy[0], 1)
                wait(dve, rk_mm, l, 1)
                link(v_.tensor_copy(r_cnt, ps[:, 1, 0:96]))
                link(tt(r_th, r_cnt[:, 80:96].unsqueeze(2).to_broadcast([P, NE, 5]),
                        step128.unsqueeze(1).to_broadcast([P, NE, 5]), ALU.is_gt))
                link(v_.tensor_reduce(r_nt, r_th, AX, ALU.add))
                link(v_.tensor_tensor_scan(r_end, r_nt, r_nt, 0.0, ALU.add, ALU.bypass))
                link(tt(r_st, r_end, r_nt, ALU.subtract))
                link(v_.scalar_tensor_tensor(out=r_pos.rearrange("p (t e) -> p t e", t=NTILE), in0=r_st.unsqueeze(1).to_broadcast([P, NTILE, NE]),
                                             scalar=float(P), in1=r_cnt[:, 0:80].rearrange("p (t e) -> p t e", t=NTILE), op0=ALU.mult, op1=ALU.add))
                link(tt(r_sl, oh12, r_pos.unsqueeze(1).to_broadcast([P, 2, 80]), ALU.mult))
                link(v_.tensor_reduce(r_slot, r_sl.rearrange("p w (t e) -> p (w t) e", t=NTILE), AX, ALU.add))
                v_.tensor_copy(slots[:, :], r_slot).then_inc(slots_rdy[0], 1)
                link(tt(r_te, r_end.unsqueeze(1).to_broadcast([P, TILES, NE]), tile_no.unsqueeze(2).to_broadcast([P, TILES, NE]), ALU.is_le))
                link(v_.tensor_reduce(r_ei, r_te, AX, ALU.add))
                link(v_.tensor_scalar(r_ei, r_ei, float(NE - 1), None, ALU.min))
                v_.tensor_copy(ints[:, 0:TILES], r_ei)
                link(tt(r_te[:, 0, 0:NT // 2], tile_no[:, 0:NT:2], r_end[:, NE - 1:NE].to_broadcast([P, NT // 2]), ALU.is_lt))
                link(v_.tensor_reduce(r_m[:, 0:1], r_te[:, 0, 0:NT // 2], AX, ALU.add))
                v_.tensor_copy(ints[:, TILES:TILES + 1], r_m[:, 0:1]).then_inc(route[0], 1)

                def rows_out(s, n):
                    dve.wait_ge(xg_tr[0], n)
                    v_.tensor_copy(xgT[:, s].rearrange("p (b k) n -> p b k n", b=2), ps[:, 0:2, :].rearrange("p b (k n) -> p b k n", k=4)).then_inc(xg_ev[0], 1)

                wait(dve, rt_x, l, 2)
                link(v_.tensor_reduce(r_sum, r_eg, AX, ALU.add))
                link(v_.tensor_scalar(r_den, r_e2, 1.0, None, ALU.add))
                link(tt(r_den, r_den, r_sum, ALU.mult))
                link(v_.reciprocal(r_w1, r_den))
                link(tt(r_w2, r_w1, r_e2, ALU.mult))

                pairs = pairs_in_use(dve, l)
                for s in range(2):
                    rows_out(s, l * NR + (s + 1))
                with dve.Fori(0, NT // 2) as it:
                    with dve.If(it < pairs):
                        def gated(s):
                            n = l * NT + it * 2 + (s + 1)
                            dve.wait_ge(eh_sg[0], n)
                            tt(hh[:, s], hh[:, s], ps[:, 2 + s, 0:DE], ALU.mult).then_inc(eh_g[0], 1)
                            dve.wait_ge(eh_g[0], n)
                            tt(hh[:, s], hh[:, s], ps[:, 2 + s, DE:2 * DE], ALU.mult).then_inc(eh_h[0], 1)

                        def act_out(s):
                            dve.wait_ge(eh_tr[0], l * NT + it * 2 + (s + 1))
                            v_.tensor_copy(ehT[:, s], ps[:, 2 + s, 0:2 * P]).then_inc(eh_ev[0], 1)

                        gated(0)
                        act_out(0)
                        gated(1)
                        rows_out(0, l * NR + it * 2 + 3)
                        act_out(1)
                        rows_out(1, l * NR + it * 2 + 4)
                    with dve.Else():
                        dve.wait_ge(xg_ev[0], l * NR + it * 2 + 2)
                        pass_pair(dve, l, it, (eh_g, 2), (eh_h, 2), (xg_ev, 2), (eh_ev, 2))

                def merge(t):
                    wait(dve, cb_tr, l, t + 1)
                    b = 2 * (t % 4)
                    x4 = xT[:, :, TO[t]:TO[t] + TM[t]].rearrange("p (b k) n -> p b k n", b=2)
                    tt(x4, x4, ps[:, b:b + 2, :].rearrange("p b (k n) -> p b k n", k=4)[:, :, :, 0:TM[t]], ALU.add).then_inc(x_in[0], 1)

                for t in range(NTILE):
                    m = TM[t]
                    wait(dve, cb_1, l, t + 1)
                    v_.scalar_tensor_tensor(out=g1[0:m, t, :], in0=g2[0:m, t, :], scalar=r_w2[0:m, t:t + 1], in1=g1[0:m, t, :],
                                            op0=ALU.mult, op1=ALU.add).then_inc(cb_2[0], 1)
                    if t:
                        merge(t - 1)
                merge(NTILE - 1)
                assert links == DVE_LINKS, links

            for t in range(NTILE):
                dve.wait_ge(y_tr[0], t + 1)
                b = 2 * (t % 2)
                v_.tensor_copy(xtok[0:TM[t], t, :].rearrange("p (b n) -> p b n", b=2), ps[0:TM[t], b:b + 2, :]).then_inc(y_ev[0], 1)



def constants():
    con = np.zeros((P, NCONST), np.float32)
    r = np.arange(P)
    con[:, K_ID:K_ID + P] = np.eye(P)
    con[:, K_NTRI:K_NTRI + P] = -(r[:, None] >= r[None, :]).astype(np.float32)
    con[:, K_STRI:K_STRI + P] = r[:, None] < r[None, :]
    inv = np.float32(10000.0) ** (-np.arange(HR, dtype=np.float32) / HR)
    for t in range(NTILE):
        pos = (r + TO[t] if t < 4 else r + PAST).astype(np.float32)
        ang = pos[:, None] * inv[None, :]
        con[:, K_COS + HR * t:K_COS + HR * t + HR] = np.cos(ang)
        con[:, K_SIN + HR * t:K_SIN + HR * t + HR] = np.sin(ang)
        con[:, K_JL + 4 * t:K_JL + 4 * t + 4] = np.arange(4) - 99.0
        con[:TM[t], K_VALID + 4 * t:K_VALID + 4 * t + 4] = 1.0
    for g, w in enumerate(WINDOWS):
        q, m = 64 * (g % 2), g // 2
        con[q:q + 64, K_INVC + 16 * m:K_INVC + 16 * m + 16] = np.float32(1.0) / np.minimum(np.arange(16) + 1, w).astype(np.float32)
    con[:, K_STEP:K_STEP + 5] = np.arange(5) * float(P)
    con[:, K_TILE:K_TILE + TILES] = np.arange(TILES)
    return con


_INS = ["x_prompt", "x_sample", "cache_mla_latent", "cache_mla_krope", "cache_sb_k", "cache_sb_v", "state_pool",
        "g_mix_norm", "w_in", "w_pool_lin", "pool_scale", "g_q_lora", "w_uq", "g_kv_lora", "w_ukv", "g_qk_q", "g_qk_k",
        "w_br_pool", "w_br_mla", "w_br_sb", "w_out", "g_ffn_norm", "w_router_group", "b_router_group",
        "w_router_expert", "b_router_expert", "w_exp_gate", "w_exp_up", "w_exp_down"]
_OUTS = [("y_p", (1, SEQ, D)), ("y_s", (1, DEC, D)),
         ("lat_p", (DEPTH, 1, SEQ, KV_LORA)), ("kr_p", (DEPTH, 1, SEQ, ROPE)), ("sbk_p", (DEPTH, 1, SEQ, SBH, 64)),
         ("sbv_p", (DEPTH, 1, SEQ, SBH, 64)), ("pool_p", (DEPTH, 1, HIST, POOL_W)),
         ("lat_s", (DEPTH, 1, DEC, KV_LORA)), ("kr_s", (DEPTH, 1, DEC, ROPE)), ("sbk_s", (DEPTH, 1, DEC, SBH, 64)),
         ("sbv_s", (DEPTH, 1, DEC, SBH, 64)), ("pool_s", (DEPTH, 1, HIST, POOL_W))]


def kernel(**inputs):
    import concourse.bacc as _bacc
    from concourse.bass_utils import run_bass_kernel_spmd as _run

    nc = _bacc.Bacc("TRN2", target_bir_lowering=False, num_devices=1)
    arrays, A, out = {}, {}, {}
    given = {name: np.ascontiguousarray(inputs[name]) for name in _INS}
    given["con"] = constants()
    given["zeros"] = np.zeros((P, D), np.float32)
    for name, a in given.items():
        arrays[f"in_{name}"] = a
        A[name] = nc.dram_tensor(f"in_{name}", a.shape, mybir.dt.from_np(a.dtype), kind="ExternalInput").ap()
    for name, shape in _OUTS:
        out[name] = nc.dram_tensor(f"out_{name}", shape, F32, kind="ExternalOutput").ap()
    hybrid_streaming_encoder(nc, A, out)
    r = _run(nc, [arrays], core_ids=[0])
    return tuple(r.results[0][f"out_{name}"] for name, _ in _OUTS)
```
